# Optimizing a Trainium2 kernel written in Bass

```python
import math
import numpy as np
import jax
import jax.numpy as jnp
from jax import lax

D_MODEL = 1024
BATCH = 1
SEQ = 256
DEPTH = 2

HEAD_DIM = 64
DIL_PAIRS = ((128, 1), (512, 4), (2048, 16))
N_DIL_GROUPS = len(DIL_PAIRS)
HEADS_PER_DIL_GROUP = 4
N_HEADS_A = N_DIL_GROUPS * HEADS_PER_DIL_GROUP
N_HEADS_B = 8
MOBA_BLOCK = 256
MOBA_TOPK = 3
MOBA_Q_CHUNK = 32
ROPE_THETA = 500000.0
ROT_DIM = HEAD_DIM // 4
D_FF = 4 * D_MODEL
CONV_WIDTH = 3
RMS_EPS = 1e-6
WIDTH_A = N_HEADS_A * HEAD_DIM
WIDTH_A_OUT = HEADS_PER_DIL_GROUP * HEAD_DIM
WIDTH_B = N_HEADS_B * HEAD_DIM
SPLIT_SIZES = (WIDTH_A, WIDTH_A, WIDTH_A, WIDTH_B, WIDTH_B, WIDTH_B, D_MODEL, D_MODEL)
D_IN = sum(SPLIT_SIZES)

kernel_name = "hybrid_dilated_moba_gated_convffn"

def rmsnorm(x, g):
    xf = x.astype(jnp.float32)
    y = xf * lax.rsqrt(jnp.mean(xf * xf, axis=-1, keepdims=True) + RMS_EPS)
    return (y * g.astype(jnp.float32)).astype(x.dtype)

def partial_rope(t, positions):
    half = ROT_DIM // 2
    inv_freq = ROPE_THETA ** (-jnp.arange(0, ROT_DIM, 2, dtype=jnp.float32) / ROT_DIM)
    ang = positions.astype(jnp.float32)[:, None, :, None] * inv_freq
    cos = jnp.cos(ang).astype(t.dtype)
    sin = jnp.sin(ang).astype(t.dtype)
    x1 = t[..., :half]
    x2 = t[..., half:ROT_DIM]
    return jnp.concatenate([x1 * cos - x2 * sin, x2 * cos + x1 * sin, t[..., ROT_DIM:]], axis=-1)

def dilated_group_attention(q, k, v, window, dilation):
    B, H, S, Dh = q.shape
    L = S // dilation
    w = window // dilation
    nb = -(-L // w)
    Lp = nb * w

    def to_sub(t):
        t = t.reshape(B, H, L, dilation, Dh).transpose(0, 1, 3, 2, 4)
        t = jnp.pad(t, ((0, 0), (0, 0), (0, 0), (0, Lp - L), (0, 0)))
        return t.reshape(B, H, dilation, nb, w, Dh)

    qb, kb, vb = to_sub(q), to_sub(k), to_sub(v)

    def with_prev(t):
        prev = jnp.concatenate([jnp.zeros_like(t[:, :, :, :1]), t[:, :, :, :-1]], axis=3)
        return jnp.concatenate([prev, t], axis=4)

    k2, v2 = with_prev(kb), with_prev(vb)
    scores = jnp.einsum('bhrnqd,bhrnkd->bhrnqk', qb, k2).astype(jnp.float32) * (Dh ** -0.5)
    qi = jnp.arange(w)[:, None]
    kj = jnp.arange(2 * w)[None, :]
    dist = w + qi - kj
    band = (dist >= 0) & (dist <= w)
    blk = jnp.arange(nb)[:, None, None]
    valid = band[None] & ((blk > 0) | (kj[None] >= w))
    scores = jnp.where(valid, scores, -jnp.inf)
    lse = jax.nn.logsumexp(scores, axis=-1)
    p = jnp.exp(scores - lse[..., None])
    out = jnp.einsum('bhrnqk,bhrnkd->bhrnqd', p.astype(v.dtype), v2)
    out = out.reshape(B, H, dilation, Lp, Dh)[:, :, :, :L].transpose(0, 1, 3, 2, 4).reshape(B, H, S, Dh)
    lse = lse.reshape(B, H, dilation, Lp)[..., :L].transpose(0, 1, 3, 2).reshape(B, H, S)
    return out, lse

def dilated_mixture_attention(qa, ka, va):
    outs, lses = [], []
    for g, (window, dilation) in enumerate(DIL_PAIRS):
        sl = slice(g * HEADS_PER_DIL_GROUP, (g + 1) * HEADS_PER_DIL_GROUP)
        o, l = dilated_group_attention(qa[:, sl], ka[:, sl], va[:, sl], window, dilation)
        outs.append(o)
        lses.append(l)
    outs = jnp.stack(outs, axis=0)
    alpha = jax.nn.softmax(jnp.stack(lses, axis=0), axis=0)
    return jnp.sum(alpha[..., None].astype(outs.dtype) * outs, axis=0)

def moba_attention(q, k, v):
    B, H, S, Dh = q.shape
    nblk = -(-S // MOBA_BLOCK)
    Sp = nblk * MOBA_BLOCK
    pad = ((0, 0), (0, 0), (0, Sp - S), (0, 0))
    q, k, v = jnp.pad(q, pad), jnp.pad(k, pad), jnp.pad(v, pad)
    kb = k.reshape(B, H, nblk, MOBA_BLOCK, Dh)
    vb = v.reshape(B, H, nblk, MOBA_BLOCK, Dh)
    k_mean = jnp.mean(kb.astype(jnp.float32), axis=3)
    n_chunks = Sp // MOBA_Q_CHUNK
    chunks_per_block = MOBA_BLOCK // MOBA_Q_CHUNK
    k_eff = min(MOBA_TOPK, nblk)
    scale = Dh ** -0.5
    qc = q.reshape(B, H, n_chunks, MOBA_Q_CHUNK, Dh).transpose(2, 0, 1, 3, 4)
    bi = jnp.arange(B)[:, None, None, None]
    hi = jnp.arange(H)[None, :, None, None]

    def one_chunk(args):
        c, q_c = args
        blk = c // chunks_per_block
        gate = jnp.einsum('bhqd,bhnd->bhqn', q_c.astype(jnp.float32), k_mean)
        past = jnp.arange(nblk) < blk
        gate = jnp.where(past, gate, -jnp.inf)
        top_val, top_idx = lax.top_k(gate, k_eff)
        sel_valid = jnp.isfinite(top_val)
        k_sel = kb[bi, hi, top_idx]
        v_sel = vb[bi, hi, top_idx].reshape(B, H, MOBA_Q_CHUNK, k_eff * MOBA_BLOCK, Dh)
        qs = q_c * scale
        s_sel = jnp.einsum('bhqd,bhqjkd->bhqjk', qs, k_sel).astype(jnp.float32)
        s_sel = jnp.where(sel_valid[..., None], s_sel, -jnp.inf).reshape(B, H, MOBA_Q_CHUNK, k_eff * MOBA_BLOCK)
        k_own = lax.dynamic_index_in_dim(kb, blk, axis=2, keepdims=False)
        v_own = lax.dynamic_index_in_dim(vb, blk, axis=2, keepdims=False)
        s_own = jnp.einsum('bhqd,bhkd->bhqk', qs, k_own).astype(jnp.float32)
        q_pos = (c % chunks_per_block) * MOBA_Q_CHUNK + jnp.arange(MOBA_Q_CHUNK)
        causal = jnp.arange(MOBA_BLOCK)[None, :] <= q_pos[:, None]
        s_own = jnp.where(causal, s_own, -jnp.inf)
        p = jax.nn.softmax(jnp.concatenate([s_sel, s_own], axis=-1), axis=-1).astype(v.dtype)
        n_sel = k_eff * MOBA_BLOCK
        return (jnp.einsum('bhqk,bhqkd->bhqd', p[..., :n_sel], v_sel)
                + jnp.einsum('bhqk,bhkd->bhqd', p[..., n_sel:], v_own))

    outs = lax.map(one_chunk, (jnp.arange(n_chunks), qc))
    return outs.transpose(1, 2, 0, 3, 4).reshape(B, H, Sp, Dh)[:, :, :S]

def conv_ffn(h, w_up, conv_w, conv_b, w_down):
    S = h.shape[1]
    u = h @ w_up
    up = jnp.pad(u, ((0, 0), (CONV_WIDTH - 1, 0), (0, 0)))
    u = sum(up[:, j:j + S, :] * conv_w[j] for j in range(CONV_WIDTH)) + conv_b
    gate, val = jnp.split(u, 2, axis=-1)
    return (jax.nn.gelu(gate, approximate=True) * val) @ w_down

def setup_inputs(seed: int = 0) -> dict:
    key = jax.random.key(seed)
    ks = jax.random.split(key, 20)
    f32 = jnp.float32

    def nrm(k, shape, fan_in):
        return jax.random.normal(k, shape, f32) * (fan_in ** -0.5)

    def gain(k):
        return 1.0 + 0.02 * jax.random.normal(k, (DEPTH, D_MODEL), f32)

    x = jax.random.normal(ks[0], (BATCH, SEQ, D_MODEL), f32)
    offsets = jax.random.randint(ks[1], (BATCH,), 0, 4096, dtype=jnp.int32)
    positions = offsets[:, None] + jnp.arange(SEQ, dtype=jnp.int32)[None, :]
    return {
        "x": x,
        "positions": positions,
        "norm_pre_mix": gain(ks[2]),
        "w_in": nrm(ks[3], (DEPTH, D_MODEL, D_IN), D_MODEL),
        "b_gate": 0.01 * jax.random.normal(ks[4], (DEPTH, 2 * D_MODEL), f32),
        "w_proj_a": nrm(ks[5], (DEPTH, WIDTH_A_OUT, D_MODEL), WIDTH_A_OUT),
        "w_proj_b": nrm(ks[6], (DEPTH, WIDTH_B, D_MODEL), WIDTH_B),
        "w_out": nrm(ks[7], (DEPTH, D_MODEL, D_MODEL), D_MODEL),
        "norm_post_mix": gain(ks[8]),
        "norm_pre_ffn": gain(ks[9]),
        "w_up": nrm(ks[10], (DEPTH, D_MODEL, 2 * D_FF), D_MODEL),
        "conv_w": nrm(ks[11], (DEPTH, CONV_WIDTH, 2 * D_FF), CONV_WIDTH),
        "conv_b": 0.01 * jax.random.normal(ks[12], (DEPTH, 2 * D_FF), f32),
        "w_down": nrm(ks[13], (DEPTH, D_FF, D_MODEL), D_FF),
        "norm_post_ffn": gain(ks[14]),
    }

def reference(x, positions, norm_pre_mix, w_in, b_gate, w_proj_a, w_proj_b, w_out, norm_post_mix,
              norm_pre_ffn, w_up, conv_w, conv_b, w_down, norm_post_ffn):
    B, S, _ = x.shape
    split_idx = np.cumsum(SPLIT_SIZES)[:-1].tolist()

    def heads(t, n_heads):
        return t.reshape(B, S, n_heads, HEAD_DIM).transpose(0, 2, 1, 3)

    def merge_heads(t):
        return t.transpose(0, 2, 1, 3).reshape(B, S, -1)

    for l in range(DEPTH):
        h = rmsnorm(x, norm_pre_mix[l])
        proj = h @ w_in[l]
        qa, ka, va, qb, kb, vb, ga, gb = jnp.split(proj, split_idx, axis=-1)
        qa = partial_rope(heads(qa, N_HEADS_A), positions)
        ka = partial_rope(heads(ka, N_HEADS_A), positions)
        qb = partial_rope(heads(qb, N_HEADS_B), positions)
        kb = partial_rope(heads(kb, N_HEADS_B), positions)
        ya = merge_heads(dilated_mixture_attention(qa, ka, heads(va, N_HEADS_A)))
        yb = merge_heads(moba_attention(qb, kb, heads(vb, N_HEADS_B)))
        gate_a = jax.nn.sigmoid(ga + b_gate[l, :D_MODEL])
        gate_b = jax.nn.sigmoid(gb + b_gate[l, D_MODEL:])
        merged = gate_a * (ya @ w_proj_a[l]) + gate_b * (yb @ w_proj_b[l])
        x = x + rmsnorm(merged @ w_out[l], norm_post_mix[l])
        h = rmsnorm(x, norm_pre_ffn[l])
        x = x + rmsnorm(conv_ffn(h, w_up[l], conv_w[l], conv_b[l], w_down[l]), norm_post_ffn[l])
    return x


_drawn_inputs = setup_inputs


def setup_inputs(seed=0):
    import zlib

    import numpy as np

    out = dict(_drawn_inputs(seed))
    spreads = {}
    factors = {'b_gate': 8.0, 'conv_b': 4.574, 'norm_post_ffn': 3.515}
    for name, (base, spread) in spreads.items():
        noise = np.random.default_rng([zlib.crc32(name.encode()), seed]).standard_normal(out[name].shape)
        drawn = base * np.exp(spread * noise) if base else spread * noise
        out[name] = jnp.asarray(drawn.astype(out[name].dtype))
    for name, factor in factors.items():
        out[name] = (out[name] * factor).astype(out[name].dtype)
    return out
```

```python
import math
from contextlib import ExitStack

import numpy as np

import concourse.bass as bass
from concourse import mybir

F32 = mybir.dt.float32
F32R = mybir.dt.float32r
BF16 = mybir.dt.bfloat16
I32 = mybir.dt.int32
ALU = mybir.AluOpType
ACT = mybir.ActivationFunctionType
AX_X = mybir.AxisListType.X

P = 128
SEQ = 256
TT = SEQ // P
D = 1024
KD = D // P
DEPTH = 2
HD = 64
HEADS_A, HEADS_B, GROUP = 12, 8, 4
NGRP_A = HEADS_A // GROUP
NGRP = (HEADS_A + HEADS_B) // GROUP
HEADS = HEADS_A + HEADS_B
GW = GROUP * HD
WIDTH_A, WIDTH_B = HEADS_A * HD, HEADS_B * HD
GATE_COL = 3 * WIDTH_A + 3 * WIDTH_B
DFF = 4 * D
NCH = DFF // P
HALF_ROT = 8
THETA = 500000.0
EPS = 1e-6
SCALE = HD ** -0.5
WINDOWS = ((128, 1), (512, 4), (2048, 16))
MASKED = -1e30

TILE = 2048
RING = 3
NTILE = 78
T_GATE, T_PA, T_PB, T_OUT, T_FFN = 15, 23, 24, 26, 30
Y = GW + WIDTH_B
KY = Y // P

C_CONV, C_CONVB, C_BGATE, C_GMIX, C_GFFN = 0, 192, 256, 272, 280
NPRM = 288
PROWS = 96

STRIDE_STEPS = 7
MASK_STEPS = 1 + 2 * NGRP + 2
ANGLE_STEPS = 1 + HALF_ROT + 2 + 3 + 1
TABLE_STEPS = ANGLE_STEPS + 2
MIX_BEFORE_EXP = 3
MIX_STEPS = 13


def build_trunk(nc, x, positions, norm_pre_mix, w_in, b_gate, w_proj_a, w_proj_b, w_out, norm_post_mix,
                norm_pre_ffn, w_up, conv_w, conv_b, w_down, norm_post_ffn, out):
    ctx = ExitStack()

    def sb(name, shape, dt=F32):
        return ctx.enter_context(nc.sbuf_tensor(name, shape, dt))

    def sem(name):
        return ctx.enter_context(nc.semaphore(name))

    w_raw = sb("w_raw", [P, RING, TILE])
    w_hi = sb("w_hi", [P, RING, TILE], F32R)
    w_lo = sb("w_lo", [P, RING, TILE], F32R)
    xs = sb("xs", [P, TT, D])
    junk = sb("junk", [P, TT, D], BF16)
    wide = sb("wide", [P, HEADS * TT * HD])
    hn = wide[:, 0:TT * D].rearrange("p (t d) -> p t d", t=TT)
    o_all = wide[:]
    hT_hi = sb("hT_hi", [P, KD, SEQ], F32R)
    hT_lo = sb("hT_lo", [P, KD, SEQ], F32R)
    post = sb("post", [P, D])
    g_post = sb("g_post", [P, 2, D])
    sumsq = sb("sumsq", [P, 4, TT])
    meansq = sb("meansq", [P, 4, TT])
    rstd = sb("rstd", [P, 4, TT])
    minus_half = sb("minus_half", [P, 1])
    qkv = sb("qkv", [P, TT, 3, GW])
    rope_t = sb("rope_t", [P, 4, TT, 2 * GROUP, HALF_ROT])
    qkT = sb("qkT", [P, 2, 2 * SEQ])
    probs = sb("probs", [P, 2, 3 * P])
    probsT = sb("probsT", [P, 2, 3 * P])
    mx = sb("mx", [P, GROUP, TT])
    nb = sb("nb", [P, GROUP, TT])
    den = sb("den", [P, GROUP, TT])
    nb_all = sb("nb_all", [P, HEADS * TT])
    den_all = sb("den_all", [P, HEADS * TT])
    mix_e = sb("mix_e", [P, HEADS_A * TT])
    mix_t = sb("mix_t", [P, 6, GROUP * TT])
    coef = sb("coef", [P, HEADS * TT])
    y = sb("y", [P, TT, Y])
    yT_hi = sb("yT_hi", [P, KY, SEQ], F32R)
    yT_lo = sb("yT_lo", [P, KY, SEQ], F32R)
    gates = sb("gates", [P, 2 * KD, SEQ])
    conv = sb("conv", [P, 2, 2 * SEQ])
    prod = sb("prod", [P, 2, SEQ])
    act_hi = sb("act_hi", [P, 2, SEQ], F32R)
    act_lo = sb("act_lo", [P, 2, SEQ], F32R)
    ident = sb("ident", [P, P])
    ident_b = sb("ident_b", [P, P], BF16)
    mask = sb("mask", [P, NGRP, 3 * P], BF16)
    dist = sb("dist", [P, 3 * P], I32)
    dist_m = sb("dist_m", [P, 3 * P], I32)
    prm_rows = sb("prm_rows", [PROWS, DEPTH, 3, P])
    prm = sb("prm", [P, DEPTH * NPRM])
    bgate2 = sb("bgate2", [P, DEPTH * 2 * KD])
    pos_i = sb("pos_i", [P, TT], I32)
    pos_f = sb("pos_f", [P, TT])
    angle = sb("angle", [P, 6, TT, HALF_ROT])
    turns = sb("turns", [P, TT, HALF_ROT], I32)
    cos = sb("cos", [P, TT, HALF_ROT])
    sin = sb("sin", [P, TT, HALF_ROT])

    ps = ctx.enter_context(nc.psum_tensor("ps", [P, 8, 512], F32))
    B_S, B_PT, B_T, B_O, B_ACC = 3, 5, 6, 7, 4

    w_landed = [sem(f"w_landed{s}") for s in range(RING)]
    hi_made = sem("hi_made")
    lo_made = sem("lo_made")
    tile_used = sem("tile_used")
    prm_landed = sem("prm_landed")
    pos_landed = sem("pos_landed")
    gpost_landed = sem("gpost_landed")
    ident_made = sem("ident_made")
    dist_made = sem("dist_made")
    stride_made = sem("stride_made")
    mask_step = sem("mask_step")
    prm_tr = sem("prm_tr")
    prm_made = sem("prm_made")
    bgate_made = sem("bgate_made")
    table_step = sem("table_step")
    sin_made = sem("sin_made")
    x_ready = [sem(f"x_ready{t}") for t in range(TT)]
    sq_done = sem("sq_done")
    mean_made = sem("mean_made")
    rstd_made = sem("rstd_made")
    h_ready = sem("h_ready")
    h_tr = sem("h_tr")
    hT_hi_made = sem("hT_hi_made")
    hT_lo_made = sem("hT_lo_made")
    proj_ev = sem("proj_ev")
    rope_step = sem("rope_step")
    rope_done = sem("rope_done")
    qk_tr = sem("qk_tr")
    qk_ev = sem("qk_ev")
    scores_done = sem("scores_done")
    mx_made = sem("mx_made")
    nb_made = sem("nb_made")
    exp_done = sem("exp_done")
    pt_done = sem("pt_done")
    pt_ev = sem("pt_ev")
    pv_done = sem("pv_done")
    o_ev = sem("o_ev")
    mix_step = sem("mix_step")
    mix_exp = sem("mix_exp")
    y_tr = sem("y_tr")
    yT_hi_made = sem("yT_hi_made")
    yT_lo_made = sem("yT_lo_made")
    gate_ev = sem("gate_ev")
    mg_done = sem("mg_done")
    mg_read = sem("mg_read")
    mg_sum = sem("mg_sum")
    mg_hi = sem("mg_hi")
    mg_lo = sem("mg_lo")
    acc0_done = sem("acc0_done")
    post_made = sem("post_made")
    affine_done = sem("affine_done")
    tap_done = sem("tap_done")
    conv_done = sem("conv_done")
    gelu_done = sem("gelu_done")
    prod_done = sem("prod_done")
    act_hi_made = sem("act_hi_made")
    act_lo_made = sem("act_lo_made")
    stored = sem("stored")

    def nth(l, j, i=0):
        return l * NTILE + i * RING + j

    def landed(eng, l, j, i=0):
        eng.wait_ge(w_landed[j % RING], (l * (NTILE // RING) + i + j // RING) * 32 + 32)

    def used(eng, l, j, i=0):
        eng.wait_ge(tile_used, nth(l, j, i) + 1 + RING)

    PRE_MIX, POST_MIX, PRE_FFN, POST_FFN = range(4)

    def norm_count(l, q, t):
        return l * 4 * TT + q * TT + t + 1

    def head_count(l, a, h):
        return l * HEADS + a * GROUP + h + 1

    block = ctx.enter_context(nc.Block())

    @block.sync
    def _(sp):
        for t in range(TT):
            sp.dma_start(xs[:, t, :], x[0, t * P:(t + 1) * P, :]).then_inc(x_ready[t], 16)

        def load(l, j, i, halves):
            sp.wait_ge(lo_made, nth(l, j, i) + 1)
            for dst, src in halves(w_raw[:, j % RING, :]):
                sp.dma_start(dst, src).then_inc(w_landed[j % RING], 16)

        def w_in_cols(l, col):
            def halves(slot):
                s = slot.rearrange("p (k n) -> p k n", k=KD)
                w = w_in[l].rearrange("(k p) n -> p k n", p=P)[:, :, bass.ds(col, GW)]
                return [(s[:, h * 4:h * 4 + 4, :], w[:, h * 4:h * 4 + 4, :]) for h in range(2)]
            return halves

        def rows(w, l, row):
            def halves(slot):
                return [(slot[:, h * D:(h + 1) * D], w[l][bass.ds(row + h * P, P), :]) for h in range(2)]
            return halves

        def up_cols(l, ch):
            def halves(slot):
                s = slot.rearrange("p (k v n) -> p k v n", k=KD, v=2)
                w = w_up[l].rearrange("(k p) n -> p k n", p=P)
                return [(s[:, :, v, :], w[:, :, bass.ds(ch * P + v * DFF, P)]) for v in range(2)]
            return halves

        with sp.Fori(0, DEPTH) as l:
            with sp.Fori(0, NGRP_A) as i:
                for c in range(3):
                    load(l, c, i, w_in_cols(l, i * GW + c * WIDTH_A))
            with sp.Fori(0, NGRP - NGRP_A) as i:
                for c in range(3):
                    load(l, 3 * NGRP_A + c, i, w_in_cols(l, i * GW + (3 * WIDTH_A + c * WIDTH_B)))
            for g in range(8):
                load(l, T_GATE + g, 0, w_in_cols(l, GATE_COL + g * GW))
            load(l, T_PA, 0, rows(w_proj_a, l, 0))
            for q in range(2):
                load(l, T_PB + q, 0, rows(w_proj_b, l, q * 2 * P))
            for q in range(4):
                load(l, T_OUT + q, 0, rows(w_out, l, q * 2 * P))
            for c in range(2):
                load(l, T_FFN + c, 0, up_cols(l, c))
            with sp.Fori(0, NCH // 2 - 1) as i:
                for c in range(2):
                    load(l, T_FFN + 2 + c, i, up_cols(l, i * 2 + (2 + c)))
                load(l, T_FFN + 4, i, rows(w_down, l, i * (2 * P)))
            load(l, NTILE - 1, 0, rows(w_down, l, (NCH - 2) * P))

        for t in range(TT):
            sp.wait_ge(x_ready[t], 16 + 2 * DEPTH)
            sp.dma_start(out[0, t * P:(t + 1) * P, :], xs[:, t, :]).then_inc(stored, 16)
        sp.wait_ge(stored, 16 * TT)

    @block.gpsimd
    def _(pool):
        def rows_of(w):
            return w.rearrange("(b p) -> b p", p=P)
        for l in range(DEPTH):
            cw = conv_w[l].rearrange("j (b p) -> (j b) p", p=P)
            for dst, src in ((prm_rows[:, l, 0, :], cw[0:PROWS, :]), (prm_rows[:, l, 1, :], cw[PROWS:2 * PROWS, :]),
                             (prm_rows[0:64, l, 2, :], rows_of(conv_b[l])), (prm_rows[64:80, l, 2, :], rows_of(b_gate[l])),
                             (prm_rows[80:88, l, 2, :], rows_of(norm_pre_mix[l])),
                             (prm_rows[88:96, l, 2, :], rows_of(norm_pre_ffn[l]))):
                pool.dma_start(dst, src).then_inc(prm_landed, 16)
        pool.dma_start(pos_i[:], positions.rearrange("o (t p) -> p (o t)", p=P),
                       allow_slow_non_contiguous=True).then_inc(pos_landed, 16)
        pool.memset(ident[:], 0.0).then_inc(mask_step, 1)
        pool.wait_ge(mask_step, 1)
        pool.affine_select(out=ident[:], in_=ident[:], pattern=[[-1, P]], compare_op=ALU.not_equal, fill=1.0,
                           base=0, channel_multiplier=1).then_inc(ident_made, 1)
        pool.iota(dist[:, 0:P], [[-1, P]], base=0, channel_multiplier=1)
        pool.iota(dist[:, P:3 * P], [[-1, 2 * P]], base=P, channel_multiplier=1).then_inc(dist_made, 1)
        pool.wait_ge(stride_made, STRIDE_STEPS)
        step = 1
        for g in range(NGRP):
            window = WINDOWS[g][0] if g < NGRP_A else SEQ
            for lo, n, base in ((0, P, 0), (P, 2 * P, P)):
                m = mask[:, g, lo:lo + n]
                pool.affine_select(out=m, in_=m, pattern=[[-1, n]], compare_op=ALU.is_ge, fill=MASKED,
                                   base=base, channel_multiplier=1).then_inc(mask_step, 1)
                step += 1
                if window < SEQ:
                    pool.wait_ge(mask_step, step)
                    pool.affine_select(out=m, in_=m, pattern=[[1, n]], compare_op=ALU.is_ge, fill=MASKED,
                                       base=window - base, channel_multiplier=-1).then_inc(mask_step, 1)
                    step += 1
        assert step == MASK_STEPS
        pool.wait_ge(table_step, TABLE_STEPS)

        def roots(l, q):
            for t in range(TT):
                pool.wait_ge(mean_made, norm_count(l, q, t))
                pool.tensor_tensor(rstd[:, q, t:t + 1], meansq[:, q, t:t + 1], minus_half[:], ALU.pow).then_inc(rstd_made, 1)

        pool.memset(minus_half[:], -0.5).then_inc(mask_step, 1)
        pool.wait_ge(mask_step, MASK_STEPS + 1)

        with pool.Fori(0, DEPTH) as l:
            roots(l, PRE_MIX)
            for t in range(TT):
                pool.wait_ge(x_ready[t], l * 2 + 16)
            for s, g in ((0, norm_post_mix), (1, norm_post_ffn)):
                pool.dma_start(g_post[:, s, :], g[bass.ds(l, 1), :].to_broadcast([P, D])).then_inc(gpost_landed, 16)
            with pool.Fori(0, NGRP) as i:
                pool.wait_ge(proj_ev, l * 15 + i * 3 + 2)
                qk = qkv[:, :, 0:2, :].rearrange("p t c (h d) -> p t (c h) d", d=HD)
                x1, x2 = qk[:, :, :, 0:HALF_ROT], qk[:, :, :, HALF_ROT:2 * HALF_ROT]
                for s, (a, tab) in enumerate(((x1, cos), (x2, sin), (x2, cos), (x1, sin))):
                    wide_tab = tab[:].rearrange("p t (o d) -> p t o d", o=1).to_broadcast([P, TT, 2 * GROUP, HALF_ROT])
                    last = pool.tensor_tensor(rope_t[:, s], a, wide_tab, ALU.mult)
                last.then_inc(rope_step, 1)
                pool.wait_ge(rope_step, l * NGRP + i + 1)
                pool.tensor_tensor(x1, rope_t[:, 0], rope_t[:, 1], ALU.subtract)
                pool.tensor_tensor(x2, rope_t[:, 2], rope_t[:, 3], ALU.add).then_inc(rope_done, 1)
                pool.wait_ge(rope_done, l * NGRP + i + 1)
            for u in range(4):
                pool.wait_ge(mg_read, l * 8 + 5 + u)
                a, b = gates[:, 2 * u:2 * u + 2, :], gates[:, KD + 2 * u:KD + 2 * u + 2, :]
                pool.tensor_tensor(a, a, b, ALU.add).then_inc(mg_sum, 1)
            roots(l, POST_MIX)
            roots(l, PRE_FFN)

            def product(i, u, first):
                pool.wait_ge(gelu_done, l * NCH + i * 2 + u + 1)
                if not first:
                    pool.wait_ge(act_lo_made, l * NCH + i * 2 + u - 1)
                pool.tensor_tensor(prod[:, u, :], conv[:, u, 0:SEQ], conv[:, u, SEQ:2 * SEQ],
                                   ALU.mult).then_inc(prod_done, 1)

            product(0, 0, True)
            product(0, 1, True)
            with pool.Fori(1, NCH // 2) as i:
                product(i, 0, False)
                product(i, 1, False)
            roots(l, POST_FFN)
        pool.wait_ge(gpost_landed, 32 * DEPTH)

    @block.scalar
    def _(act):
        def split_hi(l, j, i=0):
            landed(act, l, j, i)
            act.wait_ge(tile_used, nth(l, j, i) + 1)
            act.activation(w_hi[:, j % RING, :], w_raw[:, j % RING, :], ACT.Copy).then_inc(hi_made, 1)

        def square_x(l, q):
            for t in range(TT):
                act.wait_ge(x_ready[t], l * 2 + (16 + q // 2))
                act.activation(junk[:, t, :], xs[:, t, :], ACT.Square,
                               accum_out=sumsq[:, q, t:t + 1]).then_inc(sq_done, 1)

        def square_acc(l, q, last_tile):
            for t in range(TT):
                if t == 0:
                    act.wait_ge(acc0_done, l * 2 + q // 2 + 1)
                else:
                    used(act, l, last_tile)
                act.activation(junk[:, t, :].rearrange("p (b n) -> p b n", b=2),
                               ps[:, B_ACC + 2 * t:B_ACC + 2 * t + 2, :], ACT.Square,
                               accum_out=sumsq[:, q, t:t + 1]).then_inc(sq_done, 1)

        def norm_hi(l, s):
            for b in range(4):
                act.wait_ge(h_tr, l * 8 + (s * 4 + b + 1))
                for k in (2 * b, 2 * b + 1):
                    g = prm[:, bass.ds(l * NPRM + ((C_GFFN if s else C_GMIX) + k), 1)]
                    last = act.activation(hT_hi[:, k, :], ps[:, b, (k % 2) * SEQ:(k % 2 + 1) * SEQ], ACT.Copy, scale=g)
                last.then_inc(hT_hi_made, 1)

        def evacuate(l, i, c, first):
            used(act, l, c, i)
            if not first and c == 0:
                act.wait_ge(qk_tr, l * 10 + i * 2)
            if not first and c == 2:
                act.wait_ge(pv_done, l * HEADS + i * GROUP)
            act.activation(qkv[:, :, c, :], ps[:, c, :].rearrange("p (t n) -> p t n", t=TT),
                           ACT.Copy).then_inc(proj_ev, 1)

        def gate_tanh(l, g):
            used(act, l, T_GATE + g)
            for v in range(2):
                blk = 2 * g + v
                last = act.activation(gates[:, blk, :], ps[:, g % 3, v * SEQ:(v + 1) * SEQ], ACT.Tanh, scale=0.5,
                                      bias=bgate2[:, bass.ds(l * (2 * KD) + blk, 1)])
            last.then_inc(gate_ev, 1)

        def exponentials(l, a, h, first):
            act.wait_ge(nb_made, head_count(l, a, h))
            if not first:
                act.wait_ge(pt_done, head_count(l, a, h - 2))
            e = h % 2
            for t, lo, hi in ((0, 0, P), (1, P, 3 * P)):
                last = act.activation(probs[:, e, lo:hi], ps[:, B_S + e, lo:hi], ACT.Exp, scale=SCALE,
                                      bias=nb[:, h, t:t + 1], accum_out=den[:, h, t:t + 1])
            last.then_inc(exp_done, 1)

        def three_tiles(l, j, i, finish, attention, first=False):
            group = i - 1
            split_hi(l, j + 2, i)
            if attention:
                exponentials(l, group, 0, first)
                exponentials(l, group, 1, first)
            finish(0)
            if attention:
                exponentials(l, group, 2, False)
            split_hi(l, j + 3, i)
            if attention:
                exponentials(l, group, 3, False)
            finish(1)
            split_hi(l, j + 4, i)
            finish(2)

        act.wait_ge(table_step, ANGLE_STEPS)
        act.activation(sin[:], angle[:, 4], ACT.Sin)
        act.activation(angle[:, 5], angle[:, 4], ACT.Sin, scale=0.5).then_inc(sin_made, 1)
        act.wait_ge(prm_made, 3 * DEPTH)
        for l in range(DEPTH):
            act.mul(bgate2[:, l * 2 * KD:(l + 1) * 2 * KD], prm[:, l * NPRM + C_BGATE:l * NPRM + C_BGATE + 2 * KD],
                    0.5).then_inc(bgate_made, 1)
        act.wait_ge(bgate_made, DEPTH)

        with act.Fori(0, DEPTH) as l:
            square_x(l, PRE_MIX)
            split_hi(l, 0)
            norm_hi(l, 0)
            split_hi(l, 1)
            three_tiles(l, 0, 0, lambda c: evacuate(l, 0, c, True), False)
            three_tiles(l, 0, 1, lambda c: evacuate(l, 1, c, False), True, first=True)
            with act.Fori(2, NGRP) as i:
                three_tiles(l, 0, i, lambda c: evacuate(l, i, c, False), True)
            three_tiles(l, 0, NGRP, lambda c: gate_tanh(l, c), True)
            for g in range(3, 8):
                split_hi(l, T_GATE + g + 2)
                if g == 4:
                    act.wait_ge(mix_step, l * MIX_STEPS + MIX_BEFORE_EXP)
                    act.activation(mix_e[:], mix_e[:], ACT.Exp).then_inc(mix_exp, 1)
                gate_tanh(l, g)
                if g == 6:
                    for b in range(KY // 2):
                        act.wait_ge(y_tr, l * 3 + (b + 1))
                        act.activation(yT_hi[:, 2 * b:2 * b + 2, :], ps[:, B_S + b, :].rearrange(
                            "p (k n) -> p k n", k=2), ACT.Copy).then_inc(yT_hi_made, 1)
            split_hi(l, T_PB + 1)
            split_hi(l, T_OUT)
            for u in range(4):
                act.wait_ge(mg_sum, l * 4 + (u + 1))
                act.activation(hT_hi[:, 2 * u:2 * u + 2, :], gates[:, 2 * u:2 * u + 2, :], ACT.Copy,
                               scale=0.5).then_inc(mg_hi, 1)
            for j in range(T_OUT + 1, T_FFN + 2):
                split_hi(l, j)
            square_acc(l, POST_MIX, T_FFN - 1)
            split_hi(l, T_FFN + 2)
            square_x(l, PRE_FFN)
            norm_hi(l, 1)

            def affine(j, m, i, u):
                used(act, l, j, m)
                for v in range(2):
                    col = l * NPRM + i * 2 + (u + v * NCH)
                    last = act.activation(conv[:, u, v * SEQ:(v + 1) * SEQ], ps[:, u, v * SEQ:(v + 1) * SEQ],
                                          ACT.Identity, scale=prm[:, bass.ds(col + (C_CONV + 2 * 2 * NCH), 1)],
                                          bias=prm[:, bass.ds(col + C_CONVB, 1)])
                last.then_inc(affine_done, 1)

            def gelu(i, u):
                act.wait_ge(conv_done, l * NCH + i * 2 + (u + 1))
                act.activation(conv[:, u, 0:SEQ], conv[:, u, 0:SEQ], ACT.Gelu_apprx_tanh).then_inc(gelu_done, 1)

            def round_act(i, u):
                act.wait_ge(prod_done, l * NCH + i * 2 + (u + 1))
                act.activation(act_hi[:, u, :], prod[:, u, :], ACT.Copy).then_inc(act_hi_made, 1)

            affine(T_FFN, 0, 0, 0)
            split_hi(l, T_FFN + 3)
            gelu(0, 0)
            affine(T_FFN + 1, 0, 0, 1)
            round_act(0, 0)
            split_hi(l, T_FFN + 4)
            gelu(0, 1)

            def two_blocks(i, m, last):
                affine(T_FFN + 2, m, i, 0)
                round_act(m, 1)
                split_hi(l, T_FFN + 5, m)
                gelu(i, 0)
                affine(T_FFN + 3, m, i, 1)
                round_act(i, 0)
                if not last:
                    split_hi(l, T_FFN + 6, m)
                gelu(i, 1)
                if not last:
                    split_hi(l, T_FFN + 7, m)

            with act.Fori(1, NCH // 2 - 1) as i:
                two_blocks(i, i - 1, False)
            two_blocks(NCH // 2 - 1, NCH // 2 - 2, True)
            used(act, l, NTILE - 2)
            round_act(NCH // 2 - 1, 1)
            square_acc(l, POST_FFN, NTILE - 1)

    @block.vector
    def _(dve):
        def split_lo(l, j, i=0):
            dve.wait_ge(hi_made, nth(l, j, i) + 1)
            s = j % RING
            dve.tensor_tensor(w_lo[:, s, :], w_raw[:, s, :], w_hi[:, s, :], ALU.subtract).then_inc(lo_made, 1)

        def make_rstd(l, q, t):
            dve.wait_ge(sq_done, norm_count(l, q, t))
            dve.tensor_scalar(meansq[:, q, t:t + 1], sumsq[:, q, t:t + 1], 1.0 / D, EPS, ALU.mult,
                              ALU.add).then_inc(mean_made, 1)
            dve.wait_ge(mean_made, norm_count(l, q, t))
            dve.wait_ge(rstd_made, norm_count(l, q, t))

        def norm_rows(l, q):
            for t in range(TT):
                make_rstd(l, q, t)
                dve.tensor_scalar(hn[:, t, :], xs[:, t, :], rstd[:, q, t:t + 1], None, ALU.mult).then_inc(h_ready, 1)

        def norm_lo(l, s):
            for b in range(4):
                dve.wait_ge(hT_hi_made, l * 8 + (s * 4 + b + 1))
                for k in (2 * b, 2 * b + 1):
                    g = prm[:, bass.ds(l * NPRM + ((C_GFFN if s else C_GMIX) + k), 1)]
                    last = dve.scalar_tensor_tensor(hT_lo[:, k, :], ps[:, b, (k % 2) * SEQ:(k % 2 + 1) * SEQ], g,
                                                    hT_hi[:, k, :], ALU.mult, ALU.subtract)
                last.then_inc(hT_lo_made, 1)

        def add_normed(l, q, s):
            for t in range(TT):
                make_rstd(l, q, t)
                if t == 0 and s == 0:
                    dve.wait_ge(gpost_landed, l * 32 + 32)
                if t == 1:
                    dve.wait_ge(x_ready[0], l * 2 + (17 + s))
                dve.scalar_tensor_tensor(post[:].rearrange("p (b n) -> p b n", b=2),
                                         ps[:, B_ACC + 2 * t:B_ACC + 2 * t + 2, :], rstd[:, q, t:t + 1],
                                         g_post[:, s, :].rearrange("p (b n) -> p b n", b=2),
                                         ALU.mult, ALU.mult).then_inc(post_made, 1)
                dve.wait_ge(post_made, l * 4 + (s * 2 + t + 1))
                dve.tensor_tensor(xs[:, t, :], xs[:, t, :], post[:], ALU.add).then_inc(x_ready[t], 1)

        def take_qkT(l, a, pair):
            dve.wait_ge(qk_tr, l * 10 + a * 2 + (pair + 1))
            dve.tensor_copy(qkT[:, pair, :], ps[:, B_T, :]).then_inc(qk_ev, 1)

        def maxima(l, a, h, first):
            if h == 0 and not first:
                dve.wait_ge(o_ev, (l * NGRP + a) * 3)
            dve.wait_ge(scores_done, head_count(l, a, h))
            S = ps[:, B_S + h % 2, :]
            dve.tensor_reduce(mx[:, h, 0:1], S[:, 0:P], AX_X, ALU.max)
            dve.tensor_reduce(mx[:, h, 1:2], S[:, P:3 * P], AX_X, ALU.max).then_inc(mx_made, 1)
            dve.wait_ge(mx_made, head_count(l, a, h))
            dve.tensor_scalar(nb[:, h, :], mx[:, h, :], -SCALE, None, ALU.mult).then_inc(nb_made, 1)

        def take_probsT(l, a, h, first):
            dve.wait_ge(pt_done, head_count(l, a, h))
            if not first:
                dve.wait_ge(pv_done, head_count(l, a, h - 2))
            dve.tensor_copy(probsT[:, h % 2, :], ps[:, B_PT, 0:3 * P]).then_inc(pt_ev, 1)

        def put_away(l, a):
            dve.wait_ge(pv_done, head_count(l, a, GROUP - 1))
            n = GROUP * TT
            dve.tensor_scalar(o_all[:, bass.ds(a * (n * HD), n * HD)], ps[:, B_O, :], 1.0, None,
                              ALU.mult).then_inc(o_ev, 1)
            for to, of in ((nb_all, nb), (den_all, den)):
                dve.tensor_scalar(to[:, bass.ds(a * n, n)], of[:].rearrange("p h t -> p (h t)"), 1.0, None,
                                  ALU.mult).then_inc(o_ev, 1)

        def three_tiles(l, j, i, attention, first=False):
            group = i - 1
            if attention:
                take_qkT(l, group, 0)
            split_lo(l, j + 2, i)
            if attention:
                maxima(l, group, 0, first)
                maxima(l, group, 1, first)
                take_qkT(l, group, 1)
                take_probsT(l, group, 0, first)
                maxima(l, group, 2, first)
            split_lo(l, j + 3, i)
            if attention:
                take_probsT(l, group, 1, first)
                maxima(l, group, 3, first)
                take_probsT(l, group, 2, False)
            split_lo(l, j + 4, i)
            if attention:
                take_probsT(l, group, 3, False)
                put_away(l, group)

        dve.sem_inc(lo_made, RING)
        dve.wait_ge(dist_made, 1)
        step = 0
        for g in range(NGRP):
            dil = WINDOWS[g][1] if g < NGRP_A else 1
            if dil == 1:
                dve.memset(mask[:, g, :], 0.0).then_inc(stride_made, 1)
                step += 1
            else:
                dve.tensor_scalar(dist_m[:], dist[:], dil - 1, None, ALU.bitwise_and).then_inc(stride_made, 1)
                dve.wait_ge(stride_made, step + 1)
                dve.tensor_scalar(mask[:, g, :], dist_m[:], 0, MASKED, ALU.is_gt, ALU.mult).then_inc(stride_made, 1)
                dve.wait_ge(stride_made, step + 2)
                step += 2
        assert step == STRIDE_STEPS
        dve.wait_ge(ident_made, 1)
        dve.tensor_copy(ident_b[:], ident[:]).then_inc(ident_made, 1)

        step = 0

        def table(ins):
            nonlocal step
            ins.then_inc(table_step, 1)
            step += 1
            dve.wait_ge(table_step, step)

        dve.wait_ge(pos_landed, 16)
        table(dve.tensor_copy(pos_f[:], pos_i[:]))
        for f in range(HALF_ROT):
            inv_freq = float(np.float32(THETA ** (-f / HALF_ROT)))
            table(dve.tensor_scalar(angle[:, 0, :, f], pos_f[:], inv_freq, None, ALU.mult))
        c1 = 6.28125
        c2 = math.floor((2 * math.pi - c1) * 2 ** 20) / 2 ** 20
        c3 = 2 * math.pi - c1 - c2
        table(dve.tensor_scalar(turns[:], angle[:, 0], 1 / (2 * math.pi), None, ALU.mult))
        table(dve.tensor_copy(angle[:, 1], turns[:]))
        for s, (of, c) in enumerate(((0, c1), (2, c2), (3, c3))):
            table(dve.scalar_tensor_tensor(angle[:, 2 + s], angle[:, 1], -c, angle[:, of], ALU.mult, ALU.add))
        pi = float(np.nextafter(np.float32(math.pi), np.float32(0)))
        table(dve.tensor_scalar(angle[:, 4], angle[:, 4], pi, -pi, ALU.min, ALU.max))
        assert step == ANGLE_STEPS
        dve.wait_ge(sin_made, 1)
        table(dve.tensor_tensor(cos[:], angle[:, 5], angle[:, 5], ALU.mult))
        table(dve.tensor_scalar(cos[:], cos[:], -2.0, 1.0, ALU.mult, ALU.add))
        assert step == TABLE_STEPS

        for b in range(3 * DEPTH):
            dve.wait_ge(prm_tr, b + 1)
            dve.tensor_copy(prm[:, b * PROWS:(b + 1) * PROWS], ps[:, b, 0:PROWS]).then_inc(prm_made, 1)
        dve.wait_ge(prm_made, 3 * DEPTH)

        with dve.Fori(0, DEPTH) as l:
            norm_rows(l, PRE_MIX)
            split_lo(l, 0)
            norm_lo(l, 0)
            split_lo(l, 1)
            three_tiles(l, 0, 0, False)
            three_tiles(l, 0, 1, True, first=True)
            with dve.Fori(2, NGRP) as i:
                three_tiles(l, 0, i, True)
            three_tiles(l, 0, NGRP, True)

            n = GROUP * TT
            count = 0

            def mix(ins):
                nonlocal count
                ins.then_inc(mix_step, 1)
                count += 1
                dve.wait_ge(mix_step, l * MIX_STEPS + count)

            def of_group(buf, g, w=n):
                return buf[:, g * w:(g + 1) * w]

            def over_groups(ap):
                return ap.rearrange("p (o n) -> p o n", o=1).to_broadcast([P, NGRP_A, n])

            def by_group(buf):
                return buf[:, 0:NGRP_A * n].rearrange("p (g n) -> p g n", n=n)

            dve.wait_ge(o_ev, (l * NGRP + NGRP) * 3)
            mix(dve.tensor_tensor(mix_t[:, 0, :], of_group(nb_all, 0), of_group(nb_all, 1), ALU.min))
            mix(dve.tensor_tensor(mix_t[:, 1, :], mix_t[:, 0, :], of_group(nb_all, 2), ALU.min))
            mix(dve.tensor_tensor(by_group(mix_e), over_groups(mix_t[:, 1, :]), by_group(nb_all), ALU.subtract))
            assert count == MIX_BEFORE_EXP
            split_lo(l, T_GATE + 5)
            split_lo(l, T_GATE + 6)
            dve.wait_ge(mix_exp, l + 1)
            mix(dve.tensor_tensor(mix_t[:, 2:5, :], by_group(mix_e), by_group(den_all), ALU.mult))
            mix(dve.tensor_tensor(mix_t[:, 0, :], mix_t[:, 2, :], mix_t[:, 3, :], ALU.add))
            mix(dve.tensor_tensor(mix_t[:, 1, :], mix_t[:, 0, :], mix_t[:, 4, :], ALU.add))
            mix(dve.reciprocal(mix_t[:, 5, :], mix_t[:, 1, :]))
            mix(dve.tensor_tensor(by_group(coef), by_group(mix_e), over_groups(mix_t[:, 5, :]), ALU.mult))
            mix(dve.reciprocal(coef[:, NGRP_A * n:], den_all[:, NGRP_A * n:]))
            wa = NGRP_A * n

            def per_head(ap):
                return ap.rearrange("p (c o) -> p c o", o=1).to_broadcast([P, ap.shape[1], HD])

            def by_head(ap):
                return ap.rearrange("p (c d) -> p c d", d=HD)

            def as_y(cols, heads):
                return y[:, :, cols:cols + heads * HD].rearrange("p t (h d) -> p h t d", d=HD)

            oa = o_all[:, 0:wa * HD]
            mix(dve.tensor_tensor(by_head(oa), by_head(oa), per_head(coef[:, 0:wa]), ALU.mult))
            mix(dve.tensor_tensor(as_y(GW, HEADS_B), o_all[:, wa * HD:].rearrange("p (h t d) -> p h t d", t=TT, d=HD),
                                  coef[:, wa:].rearrange("p (h t o) -> p h t o", t=TT, o=1).to_broadcast(
                                      [P, HEADS_B, TT, HD]), ALU.mult))
            mix(dve.tensor_tensor(of_group(o_all, 0, n * HD), of_group(o_all, 0, n * HD), of_group(o_all, 1, n * HD), ALU.add))
            hthd = lambda ap: ap.rearrange("p (h t d) -> p h t d", t=TT, d=HD)
            mix(dve.tensor_tensor(as_y(0, GROUP), hthd(of_group(o_all, 0, n * HD)), hthd(of_group(o_all, 2, n * HD)), ALU.add))
            assert count == MIX_STEPS

            split_lo(l, T_GATE + 7)
            split_lo(l, T_PA)
            for b in range(KY // 2):
                dve.wait_ge(yT_hi_made, l * 3 + (b + 1))
                dve.tensor_tensor(yT_lo[:, 2 * b:2 * b + 2, :], ps[:, B_S + b, :].rearrange("p (k n) -> p k n", k=2),
                                  yT_hi[:, 2 * b:2 * b + 2, :], ALU.subtract).then_inc(yT_lo_made, 1)
            split_lo(l, T_PB)
            split_lo(l, T_PB + 1)

            dve.wait_ge(gate_ev, l * 8 + 8)

            def gated(v):
                if v == 3:
                    used(dve, l, T_PA)
                elif v == 7:
                    used(dve, l, T_PB + 1)
                else:
                    dve.wait_ge(mg_done, l * 6 + (v + 1 if v < 3 else v))
                g = gates[:, 2 * v:2 * v + 2, :]
                dve.scalar_tensor_tensor(g, g, 1.0, ps[:, v % 3, :].rearrange("p (k n) -> p k n", k=2), ALU.add,
                                         ALU.mult).then_inc(mg_read, 1)

            def merged_lo(u):
                dve.wait_ge(mg_hi, l * 4 + (u + 1))
                dve.scalar_tensor_tensor(hT_lo[:, 2 * u:2 * u + 2, :], gates[:, 2 * u:2 * u + 2, :], 0.5,
                                         hT_hi[:, 2 * u:2 * u + 2, :], ALU.mult, ALU.subtract).then_inc(mg_lo, 1)

            for v in range(5):
                gated(v)
            split_lo(l, T_OUT)
            for v in range(5, 8):
                gated(v)
                merged_lo(v - 5)
            merged_lo(3)
            for j in range(T_OUT + 1, T_FFN + 2):
                split_lo(l, j)
            add_normed(l, POST_MIX, 0)
            norm_rows(l, PRE_FFN)
            split_lo(l, T_FFN + 2)
            norm_lo(l, 1)

            def taps(i, u):
                dve.wait_ge(affine_done, l * NCH + i * 2 + (u + 1))
                for back in (1, 2):
                    for v in range(2):
                        w = prm[:, bass.ds(l * NPRM + i * 2 + (C_CONV + (2 - back) * 2 * NCH + v * NCH + u), 1)]
                        acc = conv[:, u, v * SEQ + back:(v + 1) * SEQ]
                        last = dve.scalar_tensor_tensor(acc, ps[:, u, v * SEQ:(v + 1) * SEQ - back], w, acc, ALU.mult,
                                                        ALU.add)
                    if back == 1:
                        last.then_inc(tap_done, 1)
                        dve.wait_ge(tap_done, l * NCH + i * 2 + (u + 1))
                last.then_inc(conv_done, 1)

            def rest_act(i, u):
                dve.wait_ge(act_hi_made, l * NCH + i * 2 + (u + 1))
                dve.tensor_tensor(act_lo[:, u, :], prod[:, u, :], act_hi[:, u, :], ALU.subtract).then_inc(act_lo_made, 1)

            taps(0, 0)
            split_lo(l, T_FFN + 3)
            taps(0, 1)
            rest_act(0, 0)
            split_lo(l, T_FFN + 4)

            def two_blocks(i, m, last):
                taps(i, 0)
                rest_act(m, 1)
                split_lo(l, T_FFN + 5, m)
                taps(i, 1)
                rest_act(i, 0)
                if not last:
                    split_lo(l, T_FFN + 6, m)
                    split_lo(l, T_FFN + 7, m)

            with dve.Fori(1, NCH // 2 - 1) as i:
                two_blocks(i, i - 1, False)
            two_blocks(NCH // 2 - 1, NCH // 2 - 2, True)
            rest_act(NCH // 2 - 1, 1)
            add_normed(l, POST_FFN, 1)

    @block.tensor
    def _(pe):
        def passes(out, a_hi, a_lo, b_hi, b_lo, start, stop):
            pe.matmul(out, a_hi, b_hi, start=start, stop=False)
            pe.matmul(out, a_hi, b_lo, start=False, stop=False)
            return pe.matmul(out, a_lo, b_hi, start=False, stop=stop)

        def cols(t):
            return slice(t * P, (t + 1) * P)

        def split_ready(l, j, i=0):
            pe.wait_ge(lo_made, nth(l, j, i) + 1 + RING)

        def tile(j, pattern, **dims):
            return (w_hi[:, j % RING, :].rearrange(pattern, **dims), w_lo[:, j % RING, :].rearrange(pattern, **dims))

        def turn_h(l, s):
            for t in range(TT):
                pe.wait_ge(h_ready, l * 4 + (s * 2 + t + 1))
                for k in range(KD):
                    last = pe.transpose(ps[:, k // 2, (k % 2) * SEQ + t * P:(k % 2) * SEQ + (t + 1) * P],
                                        hn[:, t, k * P:(k + 1) * P], ident[:])
                    if t == TT - 1 and k % 2:
                        last.then_inc(h_tr, 1)

        def project(l, i, c, t, first):
            if t == 0:
                split_ready(l, c, i)
                if not first:
                    pe.wait_ge(proj_ev, l * 15 + i * 3 + (c - 2))
            hi, lo = tile(c, "p (k n) -> p k n", k=KD)
            for k in range(KD):
                if first and c == 0 and t == 0 and k % 2 == 0:
                    pe.wait_ge(hT_lo_made, l * 8 + (k // 2 + 1))
                last = passes(ps[:, c, t * GW:(t + 1) * GW], hT_hi[:, k, cols(t)], hT_lo[:, k, cols(t)],
                              hi[:, k, :], lo[:, k, :], k == 0, k == KD - 1)
            if t == TT - 1:
                last.then_inc(tile_used, 1)

        def gate_block(l, g, v):
            if v == 0:
                split_ready(l, T_GATE + g)
                if g < 3:
                    pe.wait_ge(proj_ev, l * 15 + (13 + g))
                else:
                    pe.wait_ge(gate_ev, l * 8 + (g - 2))
            hi, lo = tile(T_GATE + g, "p (k n) -> p k n", k=KD)
            for k in range(KD):
                last = passes(ps[:, g % 3, v * SEQ:(v + 1) * SEQ], hi[:, k, cols(v)], lo[:, k, cols(v)],
                              hT_hi[:, k, :], hT_lo[:, k, :], k == 0, k == KD - 1)
            if v == 1:
                last.then_inc(tile_used, 1)

        def turn_qk(l, a, pair, first):
            pe.wait_ge(rope_done, l * NGRP + a + 1)
            if not first:
                pe.wait_ge(qk_ev, l * 10 + a * 2 + pair)
            for c in range(2):
                for t in range(TT):
                    last = pe.transpose(ps[:, B_T, (2 * c + t) * P:(2 * c + t + 1) * P],
                                        qkv[:, t, c, pair * P:(pair + 1) * P], ident[:])
            last.then_inc(qk_tr, 1)

        def scores(l, a, h, first):
            pe.wait_ge(qk_ev, l * 10 + a * 2 + (h // 2 + 1))
            if not first:
                pe.wait_ge(exp_done, head_count(l, a, h - 2))
            e = h % 2
            r = slice(e * HD, (e + 1) * HD)
            q, k = qkT[r, h // 2, 0:SEQ], qkT[r, h // 2, SEQ:2 * SEQ]
            for t, lo, n in ((0, 0, P), (1, P, 2 * P)):
                S = ps[:, B_S + e, lo:lo + n]
                m = mask[:].rearrange("p g n -> p (g n)")[:, bass.ds(a * (3 * P) + lo, n)]
                pe.matmul(S, ident_b[:], m, start=True, stop=False)
                last = pe.matmul(S, q[:, cols(t)], k[:, 0:n], start=False, stop=True)
            last.then_inc(scores_done, 1)

        def turn_probs(l, a, h, first):
            pe.wait_ge(exp_done, head_count(l, a, h))
            if not first:
                pe.wait_ge(pt_ev, head_count(l, a, h - 1))
            for b in range(3):
                last = pe.transpose(ps[:, B_PT, cols(b)], probs[:, h % 2, cols(b)], ident[:])
            last.then_inc(pt_done, 1)

        def times_v(l, a, h, first):
            if h == 0:
                pe.wait_ge(proj_ev, l * 15 + a * 3 + 3)
                if not first:
                    pe.wait_ge(o_ev, (l * NGRP + a) * 3)
            pe.wait_ge(pt_ev, head_count(l, a, h))
            e = h % 2
            v = slice(h * HD, (h + 1) * HD)
            o0, o1 = (ps[:, B_O, (h * TT + t) * HD:(h * TT + t + 1) * HD] for t in range(TT))
            pe.matmul(o0, probsT[:, e, cols(0)], qkv[:, 0, 2, v], start=True, stop=True)
            pe.matmul(o1, probsT[:, e, cols(1)], qkv[:, 0, 2, v], start=True, stop=False)
            pe.matmul(o1, probsT[:, e, cols(2)], qkv[:, 1, 2, v], start=False, stop=True).then_inc(pv_done, 1)

        def three_tiles(l, i, half, attention, first=False):
            a = i - 1
            if not attention:
                for c in range(3):
                    half(c, 0)
                    half(c, 1)
                return
            turn_qk(l, a, 0, first)
            half(0, 0)
            scores(l, a, 0, first)
            scores(l, a, 1, first)
            turn_qk(l, a, 1, False)
            half(0, 1)
            turn_probs(l, a, 0, first)
            scores(l, a, 2, False)
            half(1, 0)
            times_v(l, a, 0, first)
            turn_probs(l, a, 1, False)
            scores(l, a, 3, False)
            half(1, 1)
            times_v(l, a, 1, first)
            turn_probs(l, a, 2, False)
            half(2, 0)
            times_v(l, a, 2, first)
            turn_probs(l, a, 3, False)
            half(2, 1)
            times_v(l, a, 3, first)

        pe.sem_inc(tile_used, RING)
        pe.wait_ge(prm_landed, 16 * 6 * DEPTH)
        pe.wait_ge(ident_made, 2)
        for b in range(3 * DEPTH):
            pe.transpose(ps[:, b, 0:PROWS], prm_rows[:, b // 3, b % 3, :], ident[0:PROWS, 0:PROWS]).then_inc(prm_tr, 1)
        pe.wait_ge(prm_made, 3 * DEPTH)
        pe.wait_ge(mask_step, MASK_STEPS)

        with pe.Fori(0, DEPTH) as l:
            turn_h(l, 0)
            three_tiles(l, 0, lambda c, t: project(l, 0, c, t, True), False)
            three_tiles(l, 1, lambda c, t: project(l, 1, c, t, False), True, first=True)
            with pe.Fori(2, NGRP) as i:
                three_tiles(l, i, lambda c, t: project(l, i, c, t, False), True)
            three_tiles(l, NGRP, lambda c, t: gate_block(l, c, t), True)
            for g in range(3, 8):
                if g == 7:
                    pe.wait_ge(mix_step, l * MIX_STEPS + MIX_STEPS)
                    for k in range(KY):
                        for t in range(TT):
                            last = pe.transpose(ps[:, B_S + k // 2, (k % 2) * SEQ + t * P:(k % 2) * SEQ + (t + 1) * P],
                                                y[:, t, k * P:(k + 1) * P], ident[:])
                        if k % 2:
                            last.then_inc(y_tr, 1)
                gate_block(l, g, 0)
                gate_block(l, g, 1)

            pe.wait_ge(yT_lo_made, l * 3 + 3)
            for v in range(8):
                if v == 0:
                    split_ready(l, T_PA)
                if v == 4:
                    split_ready(l, T_PB + 1)
                if v < 2:
                    pe.wait_ge(gate_ev, l * 8 + (7 + v))
                elif v >= 3:
                    pe.wait_ge(mg_read, l * 8 + (v - 2))
                k0, tiles = ((0, [T_PA]), (2, [T_PB, T_PB + 1]))[v // 4]
                nk = 2 * len(tiles)
                for f in range(2):
                    blk = 2 * (v % 4) + f
                    for k in range(nk):
                        hi, lo = tile(tiles[k // 2], "p (k n) -> p k n", k=2)
                        outp = ps[:, v % 3, f * SEQ:(f + 1) * SEQ]
                        w_h, w_l = hi[:, k % 2, cols(blk)], lo[:, k % 2, cols(blk)]
                        y_h, y_l = yT_hi[:, k0 + k, :], yT_lo[:, k0 + k, :]
                        head = pe.matmul(outp, w_h, y_h, start=k == 0, stop=False)
                        if v == 4 and f == 0 and k == 0:
                            head.then_inc(tile_used, 1)
                        pe.matmul(outp, w_h, y_l, start=False, stop=False)
                        last = pe.matmul(outp, w_l, y_h, start=False, stop=k == nk - 1)
                if v == 7:
                    last.then_inc(tile_used, 2)
                elif v != 3:
                    last.then_inc(mg_done, 1)

            def accumulate(k, w_hi_k, w_lo_k, a_hi, a_lo, t, first, final):
                for h in range(2):
                    n = slice(h * 512, (h + 1) * 512)
                    last = passes(ps[:, B_ACC + 2 * t + h, :], a_hi[:, cols(t)], a_lo[:, cols(t)], w_hi_k[:, n],
                                  w_lo_k[:, n], first, final)
                return last

            for q in range(4):
                split_ready(l, T_OUT + q)
                pe.wait_ge(mg_lo, l * 4 + (q + 1))
                hi, lo = tile(T_OUT + q, "p (k n) -> p k n", k=2)
                for t in range(TT):
                    for k in range(2):
                        c = 2 * q + k
                        last = accumulate(c, hi[:, k, :], lo[:, k, :], hT_hi[:, c, :], hT_lo[:, c, :], t, c == 0, c == KD - 1)
                    if q == 3 and t == 0:
                        last.then_inc(acc0_done, 1)
                last.then_inc(tile_used, 1)

            turn_h(l, 1)

            def up(j, m, i, u, first):
                split_ready(l, j, m)
                if not first:
                    pe.wait_ge(conv_done, l * NCH + i * 2 + (u - 1))
                hi, lo = tile(j, "p (k v n) -> p k v n", k=KD, v=2)
                for v in range(2):
                    for k in range(KD):
                        if first and u == 0 and v == 0 and k % 2 == 0:
                            pe.wait_ge(hT_lo_made, l * 8 + (4 + k // 2 + 1))
                        last = passes(ps[:, u, v * SEQ:(v + 1) * SEQ], hi[:, k, v, :], lo[:, k, v, :], hT_hi[:, k, :],
                                      hT_lo[:, k, :], k == 0, k == KD - 1)
                last.then_inc(tile_used, 1)

            def down(j, m, i, u, t, first, final):
                pe.wait_ge(act_lo_made, l * NCH + i * 2 + (u + 1))
                hi, lo = tile(j, "p (k n) -> p k n", k=2)
                return accumulate(None, hi[:, u, :], lo[:, u, :], act_hi[:, u, :], act_lo[:, u, :], t, first, final)

            def two_blocks(i, m, first):
                up(T_FFN + 2, m, i, 0, False)
                split_ready(l, T_FFN + 4, m)
                for t in range(TT):
                    down(T_FFN + 4, m, m, 0, t, first, False)
                up(T_FFN + 3, m, i, 1, False)
                for t in range(TT):
                    last = down(T_FFN + 4, m, m, 1, t, False, False)
                last.then_inc(tile_used, 1)

            up(T_FFN, 0, 0, 0, True)
            up(T_FFN + 1, 0, 0, 1, True)
            two_blocks(1, 0, True)
            with pe.Fori(2, NCH // 2) as i:
                two_blocks(i, i - 1, False)
            split_ready(l, NTILE - 1)
            for t in range(TT):
                for u in range(2):
                    last = down(NTILE - 1, 0, NCH // 2 - 1, u, t, False, u == 1)
                if t == 0:
                    last.then_inc(acc0_done, 1)
            last.then_inc(tile_used, 1)

    ctx.close()


_INS = ["x", "positions", "norm_pre_mix", "w_in", "b_gate", "w_proj_a", "w_proj_b", "w_out", "norm_post_mix",
        "norm_pre_ffn", "w_up", "conv_w", "conv_b", "w_down", "norm_post_ffn"]


def kernel(**inputs):
    import numpy as _np
    import concourse.bacc as _bacc
    from concourse import mybir as _mybir
    from concourse.bass_utils import run_bass_kernel_spmd as _run

    nc = _bacc.Bacc("TRN2", target_bir_lowering=False, num_devices=1)
    arrays, args = {}, []
    for name in _INS:
        a = _np.ascontiguousarray(inputs[name])
        arrays[f"in_{name}"] = a
        args.append(nc.dram_tensor(f"in_{name}", a.shape, _mybir.dt.from_np(a.dtype), kind="ExternalInput").ap())
    o = nc.dram_tensor("out_0", (1, SEQ, D), _mybir.dt.float32, kind="ExternalOutput").ap()
    build_trunk(nc, *args, o)
    r = _run(nc, [arrays], core_ids=[0])
    return r.results[0]["out_0"]
```

```python
import math
from contextlib import ExitStack

import numpy as np

import concourse.bass as bass
from concourse import mybir

F32 = mybir.dt.float32
F32R = mybir.dt.float32r
BF16 = mybir.dt.bfloat16
I32 = mybir.dt.int32
ALU = mybir.AluOpType
ACT = mybir.ActivationFunctionType
AX_X = mybir.AxisListType.X

P = 128
SEQ = 256
TT = SEQ // P
D = 1024
KD = D // P
DEPTH = 2
HD = 64
HEADS_A, HEADS_B, GROUP = 12, 8, 4
NGRP_A = HEADS_A // GROUP
NGRP = (HEADS_A + HEADS_B) // GROUP
HEADS = HEADS_A + HEADS_B
GW = GROUP * HD
WIDTH_A, WIDTH_B = HEADS_A * HD, HEADS_B * HD
GATE_COL = 3 * WIDTH_A + 3 * WIDTH_B
DFF = 4 * D
NCH = DFF // P
HALF_ROT = 8
THETA = 500000.0
EPS = 1e-6
SCALE = HD ** -0.5
WINDOWS = ((128, 1), (512, 4), (2048, 16))
MASKED = -1e30

TILE = 2048
RING = 3
NTILE = 78
T_GATE, T_PA, T_PB, T_OUT, T_FFN = 15, 23, 24, 26, 30
Y = GW + WIDTH_B
KY = Y // P

C_CONV, C_CONVB, C_BGATE = 0, 192, 256
PROWS = (96, 96, 80)
NPRM = sum(PROWS)

MASK_STEPS = 7
CONST_STEPS = 1 + 2
ANGLE_STEPS = 1 + 1 + 2 + 3 + 1
TABLE_STEPS = ANGLE_STEPS + 2
MIX_BEFORE_EXP = 3
MIX_STEPS = 13

LAYER_FILL, TURN_FILL, FFN_FILL = 26, 2, 18


def build_trunk(nc, x, positions, norm_pre_mix, w_in, b_gate, w_proj_a, w_proj_b, w_out, norm_post_mix,
                norm_pre_ffn, w_up, conv_w, conv_b, w_down, norm_post_ffn, out):
    ctx = ExitStack()

    def sb(name, shape, dt=F32):
        return ctx.enter_context(nc.sbuf_tensor(name, shape, dt))

    def sem(name):
        return ctx.enter_context(nc.semaphore(name))

    w_raw = sb("w_raw", [P, RING, TILE])
    w_hi = sb("w_hi", [P, RING, TILE], F32R)
    w_lo = sb("w_lo", [P, RING, TILE], F32R)
    xs = sb("xs", [P, TT, D])
    junk = sb("junk", [P, TT, D], BF16)
    wide = sb("wide", [P, HEADS * TT * HD])
    hn = wide[:, 0:TT * D].rearrange("p (t d) -> p t d", t=TT)
    o_all = wide[:]
    hT_hi = sb("hT_hi", [P, KD, SEQ], F32R)
    hT_lo = sb("hT_lo", [P, KD, SEQ], F32R)
    g_pre = sb("g_pre", [P, 2, D])
    g_post = sb("g_post", [P, 2, D])
    half_x, half_acc = sb("half_x", [P, 2, TT, 2]), sb("half_acc", [P, 2, TT, 2])
    mean_x, mean_acc = sb("mean_x", [P, 2, TT]), sb("mean_acc", [P, 2, TT])
    rstd_x, rstd_acc = sb("rstd_x", [P, 2, TT]), sb("rstd_acc", [P, 2, TT])
    minus_half = sb("minus_half", [P, 1])
    qkv = sb("qkv", [P, TT, 3, GW])
    rope_t = sb("rope_t", [P, 4, TT, 2 * GROUP, HALF_ROT])
    qkT = sb("qkT", [P, 2, 2 * SEQ])
    masked = sb("masked", [P, 2, 3 * P])
    probs = sb("probs", [P, 2, 3 * P])
    probsT = sb("probsT", [P, 2, 3 * P])
    mx = sb("mx", [P, GROUP, TT])
    nb = sb("nb", [P, GROUP, TT])
    den = sb("den", [P, GROUP, TT])
    nb_all = sb("nb_all", [P, HEADS * TT])
    den_all = sb("den_all", [P, HEADS * TT])
    mix_e = sb("mix_e", [P, HEADS_A * TT])
    mix_t = sb("mix_t", [P, 6, GROUP * TT])
    coef = sb("coef", [P, HEADS * TT])
    y = sb("y", [P, TT, Y])
    yT_hi = sb("yT_hi", [P, KY, SEQ], F32R)
    yT_lo = sb("yT_lo", [P, KY, SEQ], F32R)
    gates = sb("gates", [P, 2 * KD, SEQ])
    ag = gates[:, 0:KD, :].rearrange("p k n -> p (k n)").rearrange("p (t d) -> p t d", t=TT)
    conv = sb("conv", [P, 2, 2 * SEQ])
    prod = sb("prod", [P, 2, SEQ])
    act_hi = sb("act_hi", [P, 2, SEQ], F32R)
    act_lo = sb("act_lo", [P, 2, SEQ], F32R)
    ident = sb("ident", [P, P])
    ident_b = sb("ident_b", [P, P], BF16)
    mask = sb("mask", [P, NGRP, 3 * P], BF16)
    dist = sb("dist", [P, 3 * P], I32)
    dist_m = sb("dist_m", [P, 3 * P], I32)
    prm_rows = sb("prm_rows", [PROWS[0], 3, P])
    prm = sb("prm", [P, NPRM])
    bgate2 = sb("bgate2", [P, 2 * KD])
    freq = sb("freq", [P, HALF_ROT])
    pos_i = sb("pos_i", [P, TT], I32)
    pos_f = sb("pos_f", [P, TT])
    angle = sb("angle", [P, 6, TT, HALF_ROT])
    turns = sb("turns", [P, TT, HALF_ROT], I32)
    cos = sb("cos", [P, TT, HALF_ROT])
    sin = sb("sin", [P, TT, HALF_ROT])

    ps = ctx.enter_context(nc.psum_tensor("ps", [P, 8, 512], F32))
    B_S, B_PT, B_T, B_O, B_ACC = 3, 5, 6, 7, 4

    w_landed = [sem(f"w_landed{s}") for s in range(RING)]
    hi_made = sem("hi_made")
    first_hi = sem("first_hi")
    first_lo = sem("first_lo")
    lo_made = sem("lo_made")
    tile_used = sem("tile_used")
    prm_landed = sem("prm_landed")
    pos_landed = sem("pos_landed")
    gpre_landed = [sem(f"gpre_landed{s}") for s in range(2)]
    gpost_landed = sem("gpost_landed")
    ident_made = sem("ident_made")
    freq_made = sem("freq_made")
    dist_made = sem("dist_made")
    mask_made = sem("mask_made")
    const_step = sem("const_step")
    prm_tr = sem("prm_tr")
    prm_made = sem("prm_made")
    bgate_made = sem("bgate_made")
    table_step = sem("table_step")
    sin_made = sem("sin_made")
    x_ready = [sem(f"x_ready{t}") for t in range(TT)]
    acc_sq = sem("acc_sq")
    ag_made = sem("ag_made")
    acc_mean = sem("acc_mean")
    acc_rstd = sem("acc_rstd")
    x_sq = sem("x_sq")
    x_mean = sem("x_mean")
    x_rstd = sem("x_rstd")
    h_ready = sem("h_ready")
    h_tr = sem("h_tr")
    hT_hi_made = sem("hT_hi_made")
    hT_lo_made = sem("hT_lo_made")
    proj_ev = sem("proj_ev")
    rope_step = sem("rope_step")
    rope_done = sem("rope_done")
    qk_tr = sem("qk_tr")
    qk_ev = sem("qk_ev")
    scores_done = sem("scores_done")
    masked_made = sem("masked_made")
    mx_made = sem("mx_made")
    nb_made = sem("nb_made")
    exp_done = sem("exp_done")
    pt_done = sem("pt_done")
    pt_ev = sem("pt_ev")
    pv_done = sem("pv_done")
    o_ev = sem("o_ev")
    mix_step = sem("mix_step")
    mix_exp = sem("mix_exp")
    y_tr = sem("y_tr")
    yT_hi_made = sem("yT_hi_made")
    yT_lo_made = sem("yT_lo_made")
    gate_ev = sem("gate_ev")
    mg_done = sem("mg_done")
    mg_read = sem("mg_read")
    mg_sum = sem("mg_sum")
    mg_hi = sem("mg_hi")
    mg_lo = sem("mg_lo")
    acc0_done = sem("acc0_done")
    affine_done = sem("affine_done")
    tap_done = sem("tap_done")
    conv_done = sem("conv_done")
    gelu_done = sem("gelu_done")
    prod_done = sem("prod_done")
    act_hi_made = sem("act_hi_made")
    act_lo_made = sem("act_lo_made")
    stored = sem("stored")

    def nth(l, j, i=0):
        return l * NTILE + i * RING + j

    def landed(eng, l, j, i=0):
        eng.wait_ge(w_landed[j % RING], (l * (NTILE // RING) + i + j // RING) * 32 + 32)

    def used(eng, l, j, i=0):
        eng.wait_ge(tile_used, nth(l, j, i) + 1 + RING)

    def tile_count(l, s, t):
        return l * 2 * TT + s * TT + t + 1

    def half_count(l, s, t, b):
        return l * 4 * TT + s * 2 * TT + t * 2 + b + 1

    def wait_x(eng, l, s, t, b):
        if s == 0:
            eng.wait_ge(x_ready[t], l * 4 + 16)
        else:
            eng.wait_ge(x_ready[t], l * 4 + (16 + b + 1))

    def wait_acc(eng, l, s, t):
        if t == 0:
            eng.wait_ge(acc0_done, l * 2 + s + 1)
        else:
            used(eng, l, (T_FFN, NTILE)[s] - 1)

    def half(b):
        return slice(b * D // 2, (b + 1) * D // 2)

    def branch_bank(v):
        return (v + B_ACC) % 8

    def head_count(l, a, h):
        return l * HEADS + a * GROUP + h + 1

    block = ctx.enter_context(nc.Block())

    @block.sync
    def _(sp):
        sp.dma_start(pos_i[:], positions.rearrange("o (t p) -> p (o t)", p=P),
                     allow_slow_non_contiguous=True).then_inc(pos_landed, 16)
        sp.dma_start(xs[:, 0, :], x[0, 0:P, :]).then_inc(x_ready[0], 16)

        def load(l, j, i, halves):
            sp.wait_ge(lo_made, nth(l, j, i) + 1)
            for dst, src in halves(w_raw[:, j % RING, :]):
                sp.dma_start(dst, src).then_inc(w_landed[j % RING], 16)

        def w_in_cols(l, col):
            def halves(slot):
                s = slot.rearrange("p (k n) -> p k n", k=KD)
                w = w_in[l].rearrange("(k p) n -> p k n", p=P)[:, :, bass.ds(col, GW)]
                return [(s[:, h * 4:h * 4 + 4, :], w[:, h * 4:h * 4 + 4, :]) for h in range(2)]
            return halves

        def rows(w, l, row):
            def halves(slot):
                return [(slot[:, h * D:(h + 1) * D], w[l][bass.ds(row + h * P, P), :]) for h in range(2)]
            return halves

        def up_cols(l, ch):
            def halves(slot):
                s = slot.rearrange("p (k v n) -> p k v n", k=KD, v=2)
                w = w_up[l].rearrange("(k p) n -> p k n", p=P)
                return [(s[:, :, v, :], w[:, :, bass.ds(ch * P + v * DFF, P)]) for v in range(2)]
            return halves

        def gain(l, to, g, landed):
            sp.dma_start(to, g[bass.ds(l, 1), :].to_broadcast([P, D])).then_inc(landed, 16)

        with sp.Fori(0, DEPTH) as l:
            gain(l, g_pre[:, 0, :], norm_pre_mix, gpre_landed[0])
            for c in range(3):
                load(l, c, 0, w_in_cols(l, c * WIDTH_A))
            cw = conv_w[l].rearrange("j (b p) -> (j b) p", p=P)
            for dst, src in ((prm_rows[:, 0, :], cw[0:PROWS[0], :]), (prm_rows[:, 1, :], cw[PROWS[0]:2 * PROWS[0], :]),
                             (prm_rows[0:64, 2, :], conv_b[l].rearrange("(b p) -> b p", p=P)),
                             (prm_rows[64:80, 2, :], b_gate[l].rearrange("(b p) -> b p", p=P))):
                sp.dma_start(dst, src).then_inc(prm_landed, 16)
            with sp.Fori(1, NGRP_A) as i:
                for c in range(3):
                    load(l, c, i, w_in_cols(l, i * GW + c * WIDTH_A))
            with sp.Fori(0, NGRP - NGRP_A) as i:
                for c in range(3):
                    load(l, 3 * NGRP_A + c, i, w_in_cols(l, i * GW + (3 * WIDTH_A + c * WIDTH_B)))
            gain(l, g_post[:, 0, :], norm_post_mix, gpost_landed)
            gain(l, g_pre[:, 1, :], norm_pre_ffn, gpre_landed[1])
            gain(l, g_post[:, 1, :], norm_post_ffn, gpost_landed)
            for g in range(8):
                load(l, T_GATE + g, 0, w_in_cols(l, GATE_COL + g * GW))
            load(l, T_PA, 0, rows(w_proj_a, l, 0))
            for q in range(2):
                load(l, T_PB + q, 0, rows(w_proj_b, l, q * 2 * P))
            for q in range(4):
                load(l, T_OUT + q, 0, rows(w_out, l, q * 2 * P))
            for c in range(2):
                load(l, T_FFN + c, 0, up_cols(l, c))
            with sp.Fori(0, NCH // 2 - 1) as i:
                for c in range(2):
                    load(l, T_FFN + 2 + c, i, up_cols(l, i * 2 + (2 + c)))
                load(l, T_FFN + 4, i, rows(w_down, l, i * (2 * P)))
            load(l, NTILE - 1, 0, rows(w_down, l, (NCH - 2) * P))

        for t in range(TT):
            for b in range(2):
                sp.wait_ge(x_ready[t], 16 + 4 * DEPTH - 1 + b)
                sp.dma_start(out[0, t * P:(t + 1) * P, half(b)], xs[:, t, half(b)]).then_inc(stored, 16)
        sp.wait_ge(stored, 16 * TT * 2)

    @block.gpsimd
    def _(pool):
        pool.memset(ident[:], 0.0).then_inc(const_step, 1)
        pool.wait_ge(const_step, 1)
        pool.affine_select(out=ident[:], in_=ident[:], pattern=[[-1, P]], compare_op=ALU.not_equal, fill=1.0,
                           base=0, channel_multiplier=1).then_inc(ident_made, 1)
        for f in range(HALF_ROT):
            last = pool.memset(freq[:, f:f + 1], float(np.float32(THETA ** (-f / HALF_ROT))))
        last.then_inc(freq_made, 1)
        pool.iota(dist[:, 0:P], [[-1, P]], base=0, channel_multiplier=1)
        pool.iota(dist[:, P:3 * P], [[-1, 2 * P]], base=P, channel_multiplier=1).then_inc(dist_made, 1)
        pool.wait_ge(mask_made, MASK_STEPS)
        for g, (window, _) in enumerate(WINDOWS):
            if window < SEQ:
                for lo, n, base in ((0, P, 0), (P, 2 * P, P)):
                    m = mask[:, g, lo:lo + n]
                    pool.affine_select(out=m, in_=m, pattern=[[1, n]], compare_op=ALU.is_ge, fill=MASKED,
                                       base=window - base, channel_multiplier=-1).then_inc(const_step, 1)
        pool.wait_ge(table_step, TABLE_STEPS)

        def root(l, s, t, mean, mean_made, rstd, rstd_made):
            pool.wait_ge(mean_made, tile_count(l, s, t))
            pool.tensor_tensor(rstd[:, s, t:t + 1], mean[:, s, t:t + 1], minus_half[:], ALU.pow).then_inc(rstd_made, 1)

        def root_acc(l, s, t):
            root(l, s, t, mean_acc, acc_mean, rstd_acc, acc_rstd)

        def root_x(l, s, t):
            root(l, s, t, mean_x, x_mean, rstd_x, x_rstd)

        pool.memset(minus_half[:], -0.5).then_inc(const_step, 1)
        pool.wait_ge(const_step, CONST_STEPS + 1)

        with pool.Fori(0, DEPTH) as l:
            for t in range(TT):
                root_x(l, 0, t)
            with pool.Fori(0, NGRP) as i:
                pool.wait_ge(proj_ev, l * 15 + i * 3 + 2)
                qk = qkv[:, :, 0:2, :].rearrange("p t c (h d) -> p t (c h) d", d=HD)
                x1, x2 = qk[:, :, :, 0:HALF_ROT], qk[:, :, :, HALF_ROT:2 * HALF_ROT]
                for s, (a, tab) in enumerate(((x1, cos), (x2, sin), (x2, cos), (x1, sin))):
                    wide_tab = tab[:].rearrange("p t (o d) -> p t o d", o=1).to_broadcast([P, TT, 2 * GROUP, HALF_ROT])
                    last = pool.tensor_tensor(rope_t[:, s], a, wide_tab, ALU.mult)
                last.then_inc(rope_step, 1)
                pool.wait_ge(rope_step, l * NGRP + i + 1)
                pool.tensor_tensor(x1, rope_t[:, 0], rope_t[:, 1], ALU.subtract)
                pool.tensor_tensor(x2, rope_t[:, 2], rope_t[:, 3], ALU.add).then_inc(rope_done, 1)
                pool.wait_ge(rope_done, l * NGRP + i + 1)
            for u in range(4):
                pool.wait_ge(mg_read, l * 8 + 5 + u)
                a, b = gates[:, 2 * u:2 * u + 2, :], gates[:, KD + 2 * u:KD + 2 * u + 2, :]
                pool.tensor_tensor(a, a, b, ALU.add).then_inc(mg_sum, 1)
            for t in range(TT):
                root_acc(l, 0, t)
                root_x(l, 1, t)

            def product(i, u, first):
                pool.wait_ge(gelu_done, l * NCH + i * 2 + u + 1)
                if not first:
                    pool.wait_ge(act_lo_made, l * NCH + i * 2 + u - 1)
                pool.tensor_tensor(prod[:, u, :], conv[:, u, 0:SEQ], conv[:, u, SEQ:2 * SEQ],
                                   ALU.mult).then_inc(prod_done, 1)

            product(0, 0, True)
            product(0, 1, True)
            with pool.Fori(1, NCH // 2) as i:
                product(i, 0, False)
                product(i, 1, False)
            for t in range(TT):
                root_acc(l, 1, t)

    @block.scalar
    def _(act):
        def split_hi(l, j, i=0):
            landed(act, l, j, i)
            act.wait_ge(tile_used, nth(l, j, i) + 1)
            act.activation(w_hi[:, j % RING, :], w_raw[:, j % RING, :], ACT.Copy).then_inc(hi_made, 1)

        def split_first_hi(l):
            landed(act, l, 0)
            act.wait_ge(tile_used, nth(l, 0) + 1)
            n = TILE // 2
            act.activation(w_hi[:, 0, 0:n], w_raw[:, 0, 0:n], ACT.Copy).then_inc(first_hi, 1)
            act.activation(w_hi[:, 0, n:TILE], w_raw[:, 0, n:TILE], ACT.Copy).then_inc(hi_made, 1)

        def mean_halves(l, s, t, src, to, done, ready):
            for b in range(2):
                ready(b)
                act.activation(junk[:, t, half(b)], src(b), ACT.Square, scale=D ** -0.5,
                               accum_out=to[:, s, t, b:b + 1]).then_inc(done, 1)

        def square_x(l, s, t):
            mean_halves(l, s, t, lambda b: xs[:, t, half(b)], half_x, x_sq, lambda b: wait_x(act, l, s, t, b))

        def square_acc(l, s, t):
            def ready(b):
                if b == 0:
                    wait_acc(act, l, s, t)
                else:
                    act.wait_ge(ag_made, half_count(l, s, t, 0))
            mean_halves(l, s, t, lambda b: ps[:, B_ACC + 2 * t + b, :], half_acc, acc_sq, ready)

        def norm_hi(l, s, t):
            for b in range(2):
                act.wait_ge(h_tr, half_count(l, s, t, b))
                act.activation(hT_hi[:, 4 * b:4 * b + 4, t * P:(t + 1) * P],
                               ps[:, B_ACC + 2 * t + b, :].rearrange("p (k n) -> p k n", k=4),
                               ACT.Copy).then_inc(hT_hi_made, 1)

        def evacuate(l, i, c, first):
            used(act, l, c, i)
            if not first and c == 0:
                act.wait_ge(qk_tr, l * 10 + i * 2)
            if not first and c == 2:
                act.wait_ge(pv_done, l * HEADS + i * GROUP)
            act.activation(qkv[:, :, c, :], ps[:, c, :].rearrange("p (t n) -> p t n", t=TT),
                           ACT.Copy).then_inc(proj_ev, 1)

        def gate_tanh(l, g):
            used(act, l, T_GATE + g)
            for v in range(2):
                blk = 2 * g + v
                last = act.activation(gates[:, blk, :], ps[:, g % 3, v * SEQ:(v + 1) * SEQ], ACT.Tanh, scale=0.5,
                                      bias=bgate2[:, blk:blk + 1])
            last.then_inc(gate_ev, 1)

        def exponentials(l, a, h, first):
            act.wait_ge(nb_made, head_count(l, a, h))
            if not first:
                act.wait_ge(pt_done, head_count(l, a, h - 2))
            e = h % 2
            for t, lo, hi in ((0, 0, P), (1, P, 3 * P)):
                last = act.activation(probs[:, e, lo:hi], masked[:, e, lo:hi], ACT.Exp,
                                      bias=nb[:, h, t:t + 1], accum_out=den[:, h, t:t + 1])
            last.then_inc(exp_done, 1)

        def take_qkT(l, a, pair):
            act.wait_ge(qk_tr, l * 10 + a * 2 + (pair + 1))
            act.activation(qkT[:, pair, :], ps[:, B_T, :], ACT.Copy).then_inc(qk_ev, 1)

        def take_probsT(l, a, h, first):
            act.wait_ge(pt_done, head_count(l, a, h))
            if not first:
                act.wait_ge(pv_done, head_count(l, a, h - 2))
            act.activation(probsT[:, h % 2, :], ps[:, B_PT, 0:3 * P], ACT.Copy).then_inc(pt_ev, 1)

        def three_tiles(l, j, i, finish, attention, first=False):
            group = i - 1
            if attention:
                take_qkT(l, group, 0)
            split_hi(l, j + 2, i)
            if attention:
                take_qkT(l, group, 1)
                exponentials(l, group, 0, first)
                exponentials(l, group, 1, first)
            finish(0)
            if attention:
                take_probsT(l, group, 0, first)
            split_hi(l, j + 3, i)
            if attention:
                exponentials(l, group, 2, False)
                take_probsT(l, group, 1, first)
                exponentials(l, group, 3, False)
            finish(1)
            if attention:
                take_probsT(l, group, 2, False)
            split_hi(l, j + 4, i)
            if attention:
                take_probsT(l, group, 3, False)
            finish(2)

        act.wait_ge(table_step, ANGLE_STEPS)
        act.activation(sin[:], angle[:, 4], ACT.Sin)
        act.activation(angle[:, 5], angle[:, 4], ACT.Sin, scale=0.5).then_inc(sin_made, 1)
        act.dma_start(xs[:, 1, :], x[0, P:2 * P, :]).then_inc(x_ready[1], 16)

        with act.Fori(0, DEPTH) as l:
            for t in range(TT):
                square_x(l, 0, t)
                if t == 0:
                    split_first_hi(l)
                else:
                    split_hi(l, 1)
                norm_hi(l, 0, t)
            three_tiles(l, 0, 0, lambda c: evacuate(l, 0, c, True), False)
            act.wait_ge(prm_made, l + 1)
            act.mul(bgate2[:], prm[:, C_BGATE:C_BGATE + 2 * KD], 0.5).then_inc(bgate_made, 1)
            three_tiles(l, 0, 1, lambda c: evacuate(l, 1, c, False), True, first=True)
            with act.Fori(2, NGRP) as i:
                three_tiles(l, 0, i, lambda c: evacuate(l, i, c, False), True)
            act.wait_ge(bgate_made, l + 1)
            three_tiles(l, 0, NGRP, lambda c: gate_tanh(l, c), True)
            for g in range(3, 8):
                split_hi(l, T_GATE + g + 2)
                if g == 4:
                    act.wait_ge(mix_step, l * MIX_STEPS + MIX_BEFORE_EXP)
                    act.activation(mix_e[:], mix_e[:], ACT.Exp).then_inc(mix_exp, 1)
                gate_tanh(l, g)
                if g == 6:
                    for b in range(KY // 2):
                        act.wait_ge(y_tr, l * 3 + (b + 1))
                        act.activation(yT_hi[:, 2 * b:2 * b + 2, :], ps[:, B_S + b, :].rearrange(
                            "p (k n) -> p k n", k=2), ACT.Copy).then_inc(yT_hi_made, 1)
            split_hi(l, T_PB + 1)
            split_hi(l, T_OUT)
            for u in range(4):
                if u == 3:
                    split_hi(l, T_OUT + 1)
                act.wait_ge(mg_sum, l * 4 + (u + 1))
                act.activation(hT_hi[:, 2 * u:2 * u + 2, :], gates[:, 2 * u:2 * u + 2, :], ACT.Copy,
                               scale=0.5).then_inc(mg_hi, 1)
            for j in range(T_OUT + 2, T_FFN + 1):
                split_hi(l, j)
            square_acc(l, 0, 0)
            square_x(l, 1, 0)
            square_acc(l, 0, 1)
            square_x(l, 1, 1)
            norm_hi(l, 1, 0)
            norm_hi(l, 1, 1)
            split_hi(l, T_FFN + 1)
            split_hi(l, T_FFN + 2)

            def affine(j, m, i, u, first):
                if not first:
                    act.wait_ge(prod_done, l * NCH + i * 2 + (u - 1))
                used(act, l, j, m)
                for v in range(2):
                    col = i * 2 + (u + v * NCH)
                    last = act.activation(conv[:, u, v * SEQ:(v + 1) * SEQ], ps[:, u, v * SEQ:(v + 1) * SEQ],
                                          ACT.Identity, scale=prm[:, bass.ds(col + (C_CONV + 2 * 2 * NCH), 1)],
                                          bias=prm[:, bass.ds(col + C_CONVB, 1)])
                last.then_inc(affine_done, 1)

            def gelu(i, u):
                act.wait_ge(conv_done, l * NCH + i * 2 + (u + 1))
                act.activation(conv[:, u, 0:SEQ], conv[:, u, 0:SEQ], ACT.Gelu_apprx_tanh).then_inc(gelu_done, 1)

            def round_act(i, u, to=act_hi):
                act.wait_ge(prod_done, l * NCH + i * 2 + (u + 1))
                act.activation(to[:, u, :], prod[:, u, :], ACT.Copy).then_inc(act_hi_made, 1)

            affine(T_FFN, 0, 0, 0, True)
            split_hi(l, T_FFN + 3)
            gelu(0, 0)
            affine(T_FFN + 1, 0, 0, 1, True)
            split_hi(l, T_FFN + 4)
            gelu(0, 1)

            def two_blocks(i, m, last):
                affine(T_FFN + 2, m, i, 0, False)
                round_act(m, 0)
                round_act(m, 1)
                split_hi(l, T_FFN + 5, m)
                gelu(i, 0)
                affine(T_FFN + 3, m, i, 1, False)
                if not last:
                    split_hi(l, T_FFN + 6, m)
                gelu(i, 1)
                if not last:
                    split_hi(l, T_FFN + 7, m)

            with act.Fori(1, NCH // 2 - 1) as i:
                two_blocks(i, i - 1, False)
            two_blocks(NCH // 2 - 1, NCH // 2 - 2, True)
            for u in range(2):
                round_act(NCH // 2 - 1, u, yT_hi)
            for t in range(TT):
                square_acc(l, 1, t)

    @block.vector
    def _(dve):
        def split_lo(l, j, i=0):
            dve.wait_ge(hi_made, nth(l, j, i) + 1)
            s = j % RING
            dve.tensor_tensor(w_lo[:, s, :], w_raw[:, s, :], w_hi[:, s, :], ALU.subtract).then_inc(lo_made, 1)

        def row_mean(l, s, t):
            dve.wait_ge(x_sq, half_count(l, s, t, 1))
            dve.tensor_scalar(mean_x[:, s, t:t + 1], half_x[:, s, t, 0:1], half_x[:, s, t, 1:2], EPS, ALU.add,
                              ALU.add).then_inc(x_mean, 1)

        def norm_half(l, s, t, b):
            if t == 0 and b == 0:
                dve.wait_ge(gpre_landed[s], l * 16 + 16)
            if b == 0:
                dve.wait_ge(x_rstd, tile_count(l, s, t))
            wait_x(dve, l, s, t, b)
            dve.scalar_tensor_tensor(hn[:, t, half(b)], xs[:, t, half(b)], rstd_x[:, s, t:t + 1],
                                     g_pre[:, s, half(b)], ALU.mult, ALU.mult).then_inc(h_ready, 1)

        def norm_lo(l, s, t, b):
            dve.wait_ge(hT_hi_made, half_count(l, s, t, b))
            to = (slice(None), slice(4 * b, 4 * b + 4), slice(t * P, (t + 1) * P))
            dve.tensor_tensor(hT_lo[to], ps[:, B_ACC + 2 * t + b, :].rearrange("p (k n) -> p k n", k=4), hT_hi[to],
                              ALU.subtract).then_inc(hT_lo_made, 1)

        def gain_acc(l, s, t):
            if s == 0 and t == 0:
                dve.wait_ge(gpost_landed, l * 32 + 32)
            wait_acc(dve, l, s, t)
            for n, b in enumerate((1, 0)):
                if b == 0:
                    dve.wait_ge(acc_sq, half_count(l, s, t, 0))
                dve.tensor_tensor(ag[:, t, half(b)], ps[:, B_ACC + 2 * t + b, :], g_post[:, s, half(b)],
                                  ALU.mult).then_inc(ag_made, 1)
            dve.wait_ge(acc_sq, half_count(l, s, t, 1))
            dve.tensor_scalar(mean_acc[:, s, t:t + 1], half_acc[:, s, t, 0:1], half_acc[:, s, t, 1:2], EPS, ALU.add,
                              ALU.add).then_inc(acc_mean, 1)

        def add_normed(l, s, t):
            dve.wait_ge(ag_made, half_count(l, s, t, 1))
            dve.wait_ge(acc_rstd, tile_count(l, s, t))
            for b in range(2):
                dve.scalar_tensor_tensor(xs[:, t, half(b)], ag[:, t, half(b)], rstd_acc[:, s, t:t + 1],
                                         xs[:, t, half(b)], ALU.mult, ALU.add).then_inc(x_ready[t], 1)

        def maxima(l, a, h, first):
            if h == 0 and not first:
                dve.wait_ge(o_ev, (l * NGRP + a) * 3)
            dve.wait_ge(scores_done, head_count(l, a, h))
            if not (first and h < 2):
                dve.wait_ge(exp_done, head_count(l, a, h - 2))
            e = h % 2
            dve.scalar_tensor_tensor(masked[:, e, :], ps[:, B_S + e, 0:3 * P], SCALE, mask[:].rearrange(
                "p g n -> p (g n)")[:, bass.ds(a * (3 * P), 3 * P)], ALU.mult, ALU.add).then_inc(masked_made, 1)
            dve.wait_ge(masked_made, head_count(l, a, h))
            dve.tensor_reduce(mx[:, h, 0:1], masked[:, e, 0:P], AX_X, ALU.max)
            dve.tensor_reduce(mx[:, h, 1:2], masked[:, e, P:3 * P], AX_X, ALU.max).then_inc(mx_made, 1)
            dve.wait_ge(mx_made, head_count(l, a, h))
            dve.tensor_scalar(nb[:, h, :], mx[:, h, :], -1.0, None, ALU.mult).then_inc(nb_made, 1)

        def put_away(l, a):
            dve.wait_ge(pv_done, head_count(l, a, GROUP - 1))
            n = GROUP * TT
            dve.tensor_scalar(o_all[:, bass.ds(a * (n * HD), n * HD)], ps[:, B_O, :], 1.0, None,
                              ALU.mult).then_inc(o_ev, 1)
            for to, of in ((nb_all, nb), (den_all, den)):
                dve.tensor_scalar(to[:, bass.ds(a * n, n)], of[:].rearrange("p h t -> p (h t)"), 1.0, None,
                                  ALU.mult).then_inc(o_ev, 1)

        def three_tiles(l, j, i, attention, first=False):
            group = i - 1
            if attention:
                maxima(l, group, 0, first)
                maxima(l, group, 1, first)
            split_lo(l, j + 2, i)
            if attention:
                maxima(l, group, 2, first)
            split_lo(l, j + 3, i)
            if attention:
                maxima(l, group, 3, first)
            split_lo(l, j + 4, i)
            if attention:
                put_away(l, group)

        dve.sem_inc(lo_made, RING)
        dve.wait_ge(ident_made, 1)
        dve.tensor_copy(ident_b[:], ident[:]).then_inc(ident_made, 1)

        step = 0

        def table(ins):
            nonlocal step
            ins.then_inc(table_step, 1)
            step += 1
            dve.wait_ge(table_step, step)

        dve.wait_ge(pos_landed, 16)
        dve.wait_ge(freq_made, 1)
        table(dve.tensor_copy(pos_f[:], pos_i[:]))
        table(dve.tensor_tensor(angle[:, 0], pos_f[:].rearrange("p (t o) -> p t o", o=1).to_broadcast([P, TT, HALF_ROT]),
                                freq[:].rearrange("p (o d) -> p o d", o=1).to_broadcast([P, TT, HALF_ROT]), ALU.mult))
        c1 = 6.28125
        c2 = math.floor((2 * math.pi - c1) * 2 ** 20) / 2 ** 20
        c3 = 2 * math.pi - c1 - c2
        table(dve.tensor_scalar(turns[:], angle[:, 0], 1 / (2 * math.pi), None, ALU.mult))
        table(dve.tensor_copy(angle[:, 1], turns[:]))
        for s, (of, c) in enumerate(((0, c1), (2, c2), (3, c3))):
            table(dve.scalar_tensor_tensor(angle[:, 2 + s], angle[:, 1], -c, angle[:, of], ALU.mult, ALU.add))
        pi = float(np.nextafter(np.float32(math.pi), np.float32(0)))
        table(dve.tensor_scalar(angle[:, 4], angle[:, 4], pi, -pi, ALU.min, ALU.max))
        assert step == ANGLE_STEPS
        dve.wait_ge(dist_made, 1)
        steps = 0
        for g in range(NGRP):
            dil = WINDOWS[g][1] if g < NGRP_A else 1
            if dil == 1:
                dve.tensor_scalar(mask[:, g, :], dist[:], 0, MASKED, ALU.is_lt, ALU.mult).then_inc(mask_made, 1)
                steps += 1
            else:
                dve.tensor_scalar(dist_m[:], dist[:], SEQ + dil - 1, None, ALU.bitwise_and).then_inc(mask_made, 1)
                dve.wait_ge(mask_made, steps + 1)
                dve.tensor_scalar(mask[:, g, :], dist_m[:], 0, MASKED, ALU.is_gt, ALU.mult).then_inc(mask_made, 1)
                dve.wait_ge(mask_made, steps + 2)
                steps += 2
        assert steps == MASK_STEPS

        dve.wait_ge(sin_made, 1)
        table(dve.tensor_tensor(cos[:], angle[:, 5], angle[:, 5], ALU.mult))
        table(dve.tensor_scalar(cos[:], cos[:], -2.0, 1.0, ALU.mult, ALU.add))
        assert step == TABLE_STEPS

        with dve.Fori(0, DEPTH) as l:
            for t in range(TT):
                row_mean(l, 0, t)
                norm_half(l, 0, t, 0)
                norm_half(l, 0, t, 1)
                if t == 0:
                    dve.wait_ge(first_hi, l + 1)
                    n = slice(0, TILE // 2)
                    dve.tensor_tensor(w_lo[:, 0, n], w_raw[:, 0, n], w_hi[:, 0, n], ALU.subtract).then_inc(first_lo, 1)
                norm_lo(l, 0, t, 0)
                if t == 0:
                    dve.wait_ge(hi_made, nth(l, 0) + 1)
                    n = slice(TILE // 2, TILE)
                    dve.tensor_tensor(w_lo[:, 0, n], w_raw[:, 0, n], w_hi[:, 0, n], ALU.subtract).then_inc(lo_made, 1)
                norm_lo(l, 0, t, 1)
                if t == 1:
                    split_lo(l, 1)
            three_tiles(l, 0, 0, False)
            dve.wait_ge(prm_tr, l + 1)
            dve.tensor_copy(prm[:], ps[:, B_PT, 0:NPRM]).then_inc(prm_made, 1)
            dve.wait_ge(const_step, CONST_STEPS)
            three_tiles(l, 0, 1, True, first=True)
            with dve.Fori(2, NGRP) as i:
                three_tiles(l, 0, i, True)
            three_tiles(l, 0, NGRP, True)

            n = GROUP * TT
            count = 0

            def mix(ins):
                nonlocal count
                ins.then_inc(mix_step, 1)
                count += 1
                dve.wait_ge(mix_step, l * MIX_STEPS + count)

            def of_group(buf, g, w=n):
                return buf[:, g * w:(g + 1) * w]

            def over_groups(ap):
                return ap.rearrange("p (o n) -> p o n", o=1).to_broadcast([P, NGRP_A, n])

            def by_group(buf):
                return buf[:, 0:NGRP_A * n].rearrange("p (g n) -> p g n", n=n)

            dve.wait_ge(o_ev, (l * NGRP + NGRP) * 3)
            mix(dve.tensor_tensor(mix_t[:, 0, :], of_group(nb_all, 0), of_group(nb_all, 1), ALU.min))
            mix(dve.tensor_tensor(mix_t[:, 1, :], mix_t[:, 0, :], of_group(nb_all, 2), ALU.min))
            mix(dve.tensor_tensor(by_group(mix_e), over_groups(mix_t[:, 1, :]), by_group(nb_all), ALU.subtract))
            assert count == MIX_BEFORE_EXP
            split_lo(l, T_GATE + 5)
            split_lo(l, T_GATE + 6)
            dve.wait_ge(mix_exp, l + 1)
            mix(dve.tensor_tensor(mix_t[:, 2:5, :], by_group(mix_e), by_group(den_all), ALU.mult))
            mix(dve.tensor_tensor(mix_t[:, 0, :], mix_t[:, 2, :], mix_t[:, 3, :], ALU.add))
            mix(dve.tensor_tensor(mix_t[:, 1, :], mix_t[:, 0, :], mix_t[:, 4, :], ALU.add))
            mix(dve.reciprocal(mix_t[:, 5, :], mix_t[:, 1, :]))
            mix(dve.tensor_tensor(by_group(coef), by_group(mix_e), over_groups(mix_t[:, 5, :]), ALU.mult))
            mix(dve.reciprocal(coef[:, NGRP_A * n:], den_all[:, NGRP_A * n:]))
            wa = NGRP_A * n

            def per_head(ap):
                return ap.rearrange("p (c o) -> p c o", o=1).to_broadcast([P, ap.shape[1], HD])

            def by_head(ap):
                return ap.rearrange("p (c d) -> p c d", d=HD)

            def as_y(cols, heads):
                return y[:, :, cols:cols + heads * HD].rearrange("p t (h d) -> p h t d", d=HD)

            oa = o_all[:, 0:wa * HD]
            mix(dve.tensor_tensor(by_head(oa), by_head(oa), per_head(coef[:, 0:wa]), ALU.mult))
            mix(dve.tensor_tensor(as_y(GW, HEADS_B), o_all[:, wa * HD:].rearrange("p (h t d) -> p h t d", t=TT, d=HD),
                                  coef[:, wa:].rearrange("p (h t o) -> p h t o", t=TT, o=1).to_broadcast(
                                      [P, HEADS_B, TT, HD]), ALU.mult))
            mix(dve.tensor_tensor(of_group(o_all, 0, n * HD), of_group(o_all, 0, n * HD), of_group(o_all, 1, n * HD), ALU.add))
            hthd = lambda ap: ap.rearrange("p (h t d) -> p h t d", t=TT, d=HD)
            mix(dve.tensor_tensor(as_y(0, GROUP), hthd(of_group(o_all, 0, n * HD)), hthd(of_group(o_all, 2, n * HD)), ALU.add))
            assert count == MIX_STEPS

            split_lo(l, T_GATE + 7)
            split_lo(l, T_PA)
            for b in range(KY // 2):
                dve.wait_ge(yT_hi_made, l * 3 + (b + 1))
                dve.tensor_tensor(yT_lo[:, 2 * b:2 * b + 2, :], ps[:, B_S + b, :].rearrange("p (k n) -> p k n", k=2),
                                  yT_hi[:, 2 * b:2 * b + 2, :], ALU.subtract).then_inc(yT_lo_made, 1)
            split_lo(l, T_PB)

            dve.wait_ge(gate_ev, l * 8 + 8)

            def gated(v):
                if v == 3:
                    used(dve, l, T_PA)
                elif v == 7:
                    used(dve, l, T_PB + 1)
                else:
                    dve.wait_ge(mg_done, l * 6 + (v + 1 if v < 3 else v))
                g = gates[:, 2 * v:2 * v + 2, :]
                dve.scalar_tensor_tensor(g, g, 1.0, ps[:, branch_bank(v), :].rearrange("p (k n) -> p k n", k=2), ALU.add,
                                         ALU.mult).then_inc(mg_read, 1)

            def merged_lo(u):
                dve.wait_ge(mg_hi, l * 4 + (u + 1))
                dve.scalar_tensor_tensor(hT_lo[:, 2 * u:2 * u + 2, :], gates[:, 2 * u:2 * u + 2, :], 0.5,
                                         hT_hi[:, 2 * u:2 * u + 2, :], ALU.mult, ALU.subtract).then_inc(mg_lo, 1)

            gated(0)
            split_lo(l, T_PB + 1)
            for v in range(1, 4):
                gated(v)
            split_lo(l, T_OUT)
            for v in range(4, 8):
                gated(v)
                if v > 4:
                    merged_lo(v - 5)
            split_lo(l, T_OUT + 1)
            merged_lo(3)
            for j in range(T_OUT + 2, T_FFN + 1):
                split_lo(l, j)
            gain_acc(l, 0, 0)
            add_normed(l, 0, 0)
            row_mean(l, 1, 0)
            gain_acc(l, 0, 1)
            add_normed(l, 0, 1)
            norm_half(l, 1, 0, 0)
            row_mean(l, 1, 1)
            norm_half(l, 1, 0, 1)
            norm_half(l, 1, 1, 0)
            norm_half(l, 1, 1, 1)
            for b in range(2):
                for t in range(TT):
                    norm_lo(l, 1, t, b)
            split_lo(l, T_FFN + 1)
            split_lo(l, T_FFN + 2)

            def taps(i, u):
                dve.wait_ge(affine_done, l * NCH + i * 2 + (u + 1))
                for back in (1, 2):
                    for v in range(2):
                        w = prm[:, bass.ds(i * 2 + (C_CONV + (2 - back) * 2 * NCH + v * NCH + u), 1)]
                        acc = conv[:, u, v * SEQ + back:(v + 1) * SEQ]
                        last = dve.scalar_tensor_tensor(acc, ps[:, u, v * SEQ:(v + 1) * SEQ - back], w, acc, ALU.mult,
                                                        ALU.add)
                    if back == 1:
                        last.then_inc(tap_done, 1)
                        dve.wait_ge(tap_done, l * NCH + i * 2 + (u + 1))
                last.then_inc(conv_done, 1)

            def rest_act(i, u, of=act_hi, to=act_lo):
                dve.wait_ge(act_hi_made, l * NCH + i * 2 + (u + 1))
                dve.tensor_tensor(to[:, u, :], prod[:, u, :], of[:, u, :], ALU.subtract).then_inc(act_lo_made, 1)

            taps(0, 0)
            split_lo(l, T_FFN + 3)
            taps(0, 1)
            split_lo(l, T_FFN + 4)

            def two_blocks(i, m, last):
                taps(i, 0)
                rest_act(m, 0)
                rest_act(m, 1)
                split_lo(l, T_FFN + 5, m)
                taps(i, 1)
                if not last:
                    split_lo(l, T_FFN + 6, m)
                    split_lo(l, T_FFN + 7, m)

            with dve.Fori(1, NCH // 2 - 1) as i:
                two_blocks(i, i - 1, False)
            two_blocks(NCH // 2 - 1, NCH // 2 - 2, True)
            for u in range(2):
                rest_act(NCH // 2 - 1, u, yT_hi, yT_lo)
            for t in range(TT):
                gain_acc(l, 1, t)
                add_normed(l, 1, t)

    @block.tensor
    def _(pe):
        def passes(out, a_hi, a_lo, b_hi, b_lo, start, stop):
            pe.matmul(out, a_hi, b_hi, start=start, stop=False)
            pe.matmul(out, a_hi, b_lo, start=False, stop=False)
            return pe.matmul(out, a_lo, b_hi, start=False, stop=stop)

        def cols(t):
            return slice(t * P, (t + 1) * P)

        def split_ready(l, j, i=0):
            pe.wait_ge(lo_made, nth(l, j, i) + 1 + RING)

        def tile(j, pattern, **dims):
            return (w_hi[:, j % RING, :].rearrange(pattern, **dims), w_lo[:, j % RING, :].rearrange(pattern, **dims))

        def turn_h(l, s, t):
            for k in range(KD):
                if k % 4 == 0:
                    pe.wait_ge(h_ready, half_count(l, s, t, k // 4))
                last = pe.transpose(ps[:, B_ACC + 2 * t + k // 4, cols(k % 4)], hn[:, t, k * P:(k + 1) * P], ident[:])
                if k % 4 == 3:
                    last.then_inc(h_tr, 1)

        def keep_clock(n):
            for _ in range(n):
                pe.matmul(ps[:, B_S, :], ident_b[:], ident_b[:].rearrange("p (o n) -> p o n", o=1).to_broadcast(
                    [P, 4, P]), start=True, stop=True)

        def project(l, i, c, t, first):
            halves = first and c == 0
            if t == 0:
                if halves:
                    pe.wait_ge(first_lo, l + 1)
                else:
                    split_ready(l, c, i)
                if not first:
                    pe.wait_ge(proj_ev, l * 15 + i * 3 + (c - 2))
            hi, lo = tile(c, "p (k n) -> p k n", k=KD)
            for k in range(KD):
                if halves and t == 0 and k == 4:
                    split_ready(l, 0)
                if halves and k % 4 == 0:
                    pe.wait_ge(hT_lo_made, half_count(l, 0, t, k // 4))
                last = passes(ps[:, c, t * GW:(t + 1) * GW], hT_hi[:, k, cols(t)], hT_lo[:, k, cols(t)],
                              hi[:, k, :], lo[:, k, :], k == 0, k == KD - 1)
            if t == TT - 1:
                last.then_inc(tile_used, 1)

        def gate_block(l, g, v):
            if v == 0:
                split_ready(l, T_GATE + g)
                if g < 3:
                    pe.wait_ge(proj_ev, l * 15 + (13 + g))
                else:
                    pe.wait_ge(gate_ev, l * 8 + (g - 2))
            hi, lo = tile(T_GATE + g, "p (k n) -> p k n", k=KD)
            for k in range(KD):
                last = passes(ps[:, g % 3, v * SEQ:(v + 1) * SEQ], hi[:, k, cols(v)], lo[:, k, cols(v)],
                              hT_hi[:, k, :], hT_lo[:, k, :], k == 0, k == KD - 1)
            if v == 1:
                last.then_inc(tile_used, 1)

        def turn_qk(l, a, pair, first):
            pe.wait_ge(rope_done, l * NGRP + a + 1)
            if not first:
                pe.wait_ge(qk_ev, l * 10 + a * 2 + pair)
            for c in range(2):
                for t in range(TT):
                    last = pe.transpose(ps[:, B_T, (2 * c + t) * P:(2 * c + t + 1) * P],
                                        qkv[:, t, c, pair * P:(pair + 1) * P], ident[:])
            last.then_inc(qk_tr, 1)

        def scores(l, a, h, first):
            pe.wait_ge(qk_ev, l * 10 + a * 2 + (h // 2 + 1))
            if not first:
                pe.wait_ge(masked_made, head_count(l, a, h - 2))
            e = h % 2
            r = slice(e * HD, (e + 1) * HD)
            q, k = qkT[r, h // 2, 0:SEQ], qkT[r, h // 2, SEQ:2 * SEQ]
            for t, lo, n in ((0, 0, P), (1, P, 2 * P)):
                last = pe.matmul(ps[:, B_S + e, lo:lo + n], q[:, cols(t)], k[:, 0:n], start=True, stop=True)
            last.then_inc(scores_done, 1)

        def turn_probs(l, a, h, first):
            pe.wait_ge(exp_done, head_count(l, a, h))
            if first:
                pe.wait_ge(prm_made, l + 1)
            else:
                pe.wait_ge(pt_ev, head_count(l, a, h - 1))
            for b in range(3):
                last = pe.transpose(ps[:, B_PT, cols(b)], probs[:, h % 2, cols(b)], ident[:])
            last.then_inc(pt_done, 1)

        def times_v(l, a, h, first):
            if h == 0:
                pe.wait_ge(proj_ev, l * 15 + a * 3 + 3)
                if not first:
                    pe.wait_ge(o_ev, (l * NGRP + a) * 3)
            pe.wait_ge(pt_ev, head_count(l, a, h))
            e = h % 2
            v = slice(h * HD, (h + 1) * HD)
            o0, o1 = (ps[:, B_O, (h * TT + t) * HD:(h * TT + t + 1) * HD] for t in range(TT))
            pe.matmul(o0, probsT[:, e, cols(0)], qkv[:, 0, 2, v], start=True, stop=True)
            pe.matmul(o1, probsT[:, e, cols(1)], qkv[:, 0, 2, v], start=True, stop=False)
            pe.matmul(o1, probsT[:, e, cols(2)], qkv[:, 1, 2, v], start=False, stop=True).then_inc(pv_done, 1)

        def three_tiles(l, i, half, first=False):
            a = i - 1
            turn_qk(l, a, 0, first)
            half(0, 0)
            scores(l, a, 0, first)
            scores(l, a, 1, first)
            turn_qk(l, a, 1, False)
            half(0, 1)
            turn_probs(l, a, 0, first)
            scores(l, a, 2, False)
            half(1, 0)
            times_v(l, a, 0, first)
            turn_probs(l, a, 1, False)
            scores(l, a, 3, False)
            half(1, 1)
            times_v(l, a, 1, first)
            turn_probs(l, a, 2, False)
            half(2, 0)
            times_v(l, a, 2, first)
            turn_probs(l, a, 3, False)
            half(2, 1)
            times_v(l, a, 3, first)

        pe.sem_inc(tile_used, RING)
        pe.wait_ge(ident_made, 2)

        with pe.Fori(0, DEPTH) as l:
            keep_clock(LAYER_FILL)
            turn_h(l, 0, 0)
            keep_clock(TURN_FILL)
            project(l, 0, 0, 0, True)
            turn_h(l, 0, 1)
            project(l, 0, 0, 1, True)
            for c in (1, 2):
                for t in range(TT):
                    project(l, 0, c, t, True)
            pe.wait_ge(prm_landed, l * 64 + 64)
            at = 0
            for b, n in enumerate(PROWS):
                last = pe.transpose(ps[:, B_PT, at:at + n], prm_rows[0:n, b, :], ident[0:n, 0:n])
                at += n
            last.then_inc(prm_tr, 1)
            three_tiles(l, 1, lambda c, t: project(l, 1, c, t, False), first=True)
            with pe.Fori(2, NGRP) as i:
                three_tiles(l, i, lambda c, t: project(l, i, c, t, False))
            three_tiles(l, NGRP, lambda c, t: gate_block(l, c, t))
            for g in range(3, 8):
                if g == 7:
                    pe.wait_ge(mix_step, l * MIX_STEPS + MIX_STEPS)
                    for k in range(KY):
                        for t in range(TT):
                            last = pe.transpose(ps[:, B_S + k // 2, (k % 2) * SEQ + t * P:(k % 2) * SEQ + (t + 1) * P],
                                                y[:, t, k * P:(k + 1) * P], ident[:])
                        if k % 2:
                            last.then_inc(y_tr, 1)
                gate_block(l, g, 0)
                gate_block(l, g, 1)

            pe.wait_ge(yT_lo_made, l * 3 + 3)
            for v in range(8):
                if v == 0:
                    split_ready(l, T_PA)
                if v == 4:
                    split_ready(l, T_PB + 1)
                    pe.wait_ge(gate_ev, l * 8 + 8)
                k0, tiles = ((0, [T_PA]), (2, [T_PB, T_PB + 1]))[v // 4]
                nk = 2 * len(tiles)
                for f in range(2):
                    blk = 2 * (v % 4) + f
                    for k in range(nk):
                        hi, lo = tile(tiles[k // 2], "p (k n) -> p k n", k=2)
                        outp = ps[:, branch_bank(v), f * SEQ:(f + 1) * SEQ]
                        w_h, w_l = hi[:, k % 2, cols(blk)], lo[:, k % 2, cols(blk)]
                        y_h, y_l = yT_hi[:, k0 + k, :], yT_lo[:, k0 + k, :]
                        last = passes(outp, w_h, w_l, y_h, y_l, k == 0, k == nk - 1)
                if v % 4 == 3:
                    last.then_inc(tile_used, len(tiles))
                else:
                    last.then_inc(mg_done, 1)

            def accumulate(w_hi_k, w_lo_k, a_hi, a_lo, t, first, final):
                for h in range(2):
                    n = slice(h * 512, (h + 1) * 512)
                    last = passes(ps[:, B_ACC + 2 * t + h, :], a_hi[:, cols(t)], a_lo[:, cols(t)], w_hi_k[:, n],
                                  w_lo_k[:, n], first, final)
                return last

            pe.wait_ge(mg_read, l * 8 + 4)

            def out_rows(q, t):
                hi, lo = tile(T_OUT + q, "p (k n) -> p k n", k=2)
                for k in range(2):
                    c = 2 * q + k
                    last = accumulate(hi[:, k, :], lo[:, k, :], hT_hi[:, c, :], hT_lo[:, c, :], t, c == 0, c == KD - 1)
                if t == 1:
                    last.then_inc(tile_used, 1)
                elif q == 3:
                    last.then_inc(acc0_done, 1)

            for q, t in ((0, 0), (0, 1), (1, 0), (1, 1), (2, 0), (3, 0), (2, 1), (3, 1)):
                if t == 0:
                    split_ready(l, T_OUT + q)
                    pe.wait_ge(mg_lo, l * 4 + (q + 1))
                out_rows(q, t)

            keep_clock(FFN_FILL)
            turn_h(l, 1, 0)
            turn_h(l, 1, 1)

            def up(j, m, i, u, first):
                split_ready(l, j, m)
                if not first:
                    pe.wait_ge(conv_done, l * NCH + i * 2 + (u - 1))
                hi, lo = tile(j, "p (k v n) -> p k v n", k=KD, v=2)
                for v in range(2):
                    for k in range(KD):
                        if first and u == 0 and v == 0 and k % 4 == 0:
                            pe.wait_ge(hT_lo_made, half_count(l, 1, 0, 0) + (1 if k == 0 else 3))
                        last = passes(ps[:, u, v * SEQ:(v + 1) * SEQ], hi[:, k, v, :], lo[:, k, v, :], hT_hi[:, k, :],
                                      hT_lo[:, k, :], k == 0, k == KD - 1)
                last.then_inc(tile_used, 1)

            def down(j, m, i, u, t, first, final, a_hi=act_hi, a_lo=act_lo):
                pe.wait_ge(act_lo_made, l * NCH + i * 2 + (u + 1))
                hi, lo = tile(j, "p (k n) -> p k n", k=2)
                return accumulate(hi[:, u, :], lo[:, u, :], a_hi[:, u, :], a_lo[:, u, :], t, first, final)

            def two_blocks(i, m, first):
                up(T_FFN + 2, m, i, 0, False)
                up(T_FFN + 3, m, i, 1, False)
                split_ready(l, T_FFN + 4, m)
                for u in range(2):
                    for t in range(TT):
                        last = down(T_FFN + 4, m, m, u, t, first and u == 0, False)
                last.then_inc(tile_used, 1)

            up(T_FFN, 0, 0, 0, True)
            up(T_FFN + 1, 0, 0, 1, True)
            two_blocks(1, 0, True)
            with pe.Fori(2, NCH // 2) as i:
                two_blocks(i, i - 1, False)
            split_ready(l, NTILE - 1)
            for t in range(TT):
                for u in range(2):
                    last = down(NTILE - 1, 0, NCH // 2 - 1, u, t, False, u == 1, yT_hi, yT_lo)
                if t == 0:
                    last.then_inc(acc0_done, 1)
            last.then_inc(tile_used, 1)

    ctx.close()


_INS = ["x", "positions", "norm_pre_mix", "w_in", "b_gate", "w_proj_a", "w_proj_b", "w_out", "norm_post_mix",
        "norm_pre_ffn", "w_up", "conv_w", "conv_b", "w_down", "norm_post_ffn"]


def kernel(**inputs):
    import numpy as _np
    import concourse.bacc as _bacc
    from concourse import mybir as _mybir
    from concourse.bass_utils import run_bass_kernel_spmd as _run

    nc = _bacc.Bacc("TRN2", target_bir_lowering=False, num_devices=1)
    arrays, args = {}, []
    for name in _INS:
        a = _np.ascontiguousarray(inputs[name])
        arrays[f"in_{name}"] = a
        args.append(nc.dram_tensor(f"in_{name}", a.shape, _mybir.dt.from_np(a.dtype), kind="ExternalInput").ap())
    o = nc.dram_tensor("out_0", (1, SEQ, D), _mybir.dt.float32, kind="ExternalOutput").ap()
    build_trunk(nc, *args, o)
    r = _run(nc, [arrays], core_ids=[0])
    return r.results[0]["out_0"]
```
